# Optimizing a Trainium2 kernel written in Bass

```python
import jax, jax.numpy as jnp
from jax import lax
import numpy as np
import math

D_MODEL = 1024
BATCH = 1
SEQ = 256
DEPTH = 1

CHUNK = 64
D_PLE = 256
D_FF = 2816
D_CONV = 512
CONV_WIDTH = 31
N_HEADS_GLA = 4
D_GLA_K = 256
D_GLA_V = 512
HEAD_K = D_GLA_K // N_HEADS_GLA
HEAD_V = D_GLA_V // N_HEADS_GLA
GATE_RANK = 16
GATE_TAU = 16.0
D_MIX = D_CONV + D_GLA_V
D_IN = 2 * D_CONV + 2 * D_GLA_K + 2 * D_GLA_V + GATE_RANK
EPS = 1e-6
SPLIT_POINTS = (
    D_CONV,
    2 * D_CONV,
    2 * D_CONV + D_GLA_K,
    2 * D_CONV + 2 * D_GLA_K,
    2 * D_CONV + 2 * D_GLA_K + D_GLA_V,
    2 * D_CONV + 2 * D_GLA_K + 2 * D_GLA_V,
)


def _rmsnorm(x, g):
    xf = x.astype(jnp.float32)
    y = xf * lax.rsqrt(jnp.mean(xf * xf, axis=-1, keepdims=True) + EPS)
    return (y * g.astype(jnp.float32)).astype(x.dtype)

def _layernorm(x, g, b):
    xf = x.astype(jnp.float32)
    mu = jnp.mean(xf, axis=-1, keepdims=True)
    var = jnp.mean(jnp.square(xf - mu), axis=-1, keepdims=True)
    y = (xf - mu) * lax.rsqrt(var + EPS)
    return (y * g.astype(jnp.float32) + b.astype(jnp.float32)).astype(x.dtype)

def _swiglu(x, w_in, w_out):
    gate, up = jnp.split(x @ w_in, 2, axis=-1)
    return (jax.nn.silu(gate) * up) @ w_out

def _conv_module(a, b, w_dw, b_dw, ln_g, ln_b):
    glu = a * jax.nn.sigmoid(b)
    y = lax.conv_general_dilated(
        glu, w_dw[:, None, :],
        window_strides=(1,),
        padding=((CONV_WIDTH - 1, 0),),
        dimension_numbers=("NWC", "WIO", "NWC"),
        feature_group_count=D_CONV,
    ) + b_dw
    return jax.nn.silu(_layernorm(y, ln_g, ln_b))

def _to_chunks(t, n_heads):
    bsz, seq, width = t.shape
    return t.reshape(bsz, seq // CHUNK, CHUNK, n_heads, width // n_heads).transpose(0, 1, 3, 2, 4)

def _gla(q, k, v, r, g_lr, w_gate_up, b_gate, o_norm):
    bsz, seq, _ = q.shape
    f32 = jnp.float32
    log_a = jax.nn.log_sigmoid((g_lr @ w_gate_up + b_gate).astype(f32)) / GATE_TAU
    qc = _to_chunks(q.astype(f32), N_HEADS_GLA) * (HEAD_K ** -0.5)
    kc = _to_chunks(k.astype(f32), N_HEADS_GLA)
    vc = _to_chunks(v.astype(f32), N_HEADS_GLA)
    cum = jnp.cumsum(_to_chunks(log_a, N_HEADS_GLA), axis=3)
    e_pos = jnp.exp(cum)
    e_neg = jnp.exp(-cum)
    q_dec = qc * e_pos
    a_low = jnp.einsum("bnhtd,bnhsd->bnhts", q_dec, kc * e_neg)
    a_up = jnp.einsum("bnhtd,bnhsd->bnhts", qc * e_neg, kc * e_pos)
    pos = jnp.arange(CHUNK)
    scores = jnp.where(pos[:, None] >= pos[None, :], a_low, a_up)
    o_intra = jnp.einsum("bnhts,bnhsv->bnhtv", scores, vc)
    cum_end = cum[:, :, :, -1:, :]
    kv = jnp.einsum("bnhsd,bnhsv->bnhdv", kc * jnp.exp(cum_end - cum), vc)
    decay = jnp.exp(cum_end[:, :, :, 0, :])

    def step(state, inp):
        dec, kv_c = inp
        return dec[..., None] * state + kv_c, state

    s0 = jnp.zeros((bsz, N_HEADS_GLA, HEAD_K, HEAD_V), f32)
    _, s_prev = lax.scan(step, s0, (jnp.moveaxis(decay, 1, 0), jnp.moveaxis(kv, 1, 0)))
    s_prev = jnp.moveaxis(s_prev, 0, 1)
    o_inter = jnp.einsum("bnhtd,bnhdv->bnhtv", q_dec, s_prev)
    o = (o_intra + o_inter).transpose(0, 1, 3, 2, 4).reshape(bsz, seq, N_HEADS_GLA, HEAD_V)
    o = o * lax.rsqrt(jnp.mean(o * o, axis=-1, keepdims=True) + EPS)
    o = o * o_norm.astype(f32).reshape(N_HEADS_GLA, HEAD_V)
    return (o.reshape(bsz, seq, D_GLA_V) * jax.nn.silu(r.astype(f32))).astype(q.dtype)

def first_inputs(seed: int = 0) -> dict:
    key = jax.random.key(seed)
    ks = jax.random.split(key, 24)
    f32 = jnp.float32

    def w(k, shape, fan_in):
        return jax.random.normal(k, shape, f32) * (fan_in ** -0.5)

    def gain(k, shape):
        return 1.0 + 0.05 * jax.random.normal(k, shape, f32)

    def bias(k, shape, scale=0.02):
        return scale * jax.random.normal(k, shape, f32)

    return {
        "x": jax.random.normal(ks[0], (BATCH, SEQ, D_MODEL), f32),
        "p": jax.random.normal(ks[1], (DEPTH, BATCH, SEQ, D_PLE), f32),
        "ffn1_norm": gain(ks[2], (DEPTH, D_MODEL)),
        "ffn1_w_in": w(ks[3], (DEPTH, D_MODEL, 2 * D_FF), D_MODEL),
        "ffn1_w_out": w(ks[4], (DEPTH, D_FF, D_MODEL), D_FF),
        "mix_norm": gain(ks[5], (DEPTH, D_MODEL)),
        "w_in": w(ks[6], (DEPTH, D_MODEL, D_IN), D_MODEL),
        "conv_w": w(ks[7], (DEPTH, CONV_WIDTH, D_CONV), CONV_WIDTH),
        "conv_b": bias(ks[8], (DEPTH, D_CONV)),
        "conv_ln_g": gain(ks[9], (DEPTH, D_CONV)),
        "conv_ln_b": bias(ks[10], (DEPTH, D_CONV)),
        "gate_w_up": w(ks[11], (DEPTH, GATE_RANK, D_GLA_K), GATE_RANK),
        "gate_b": bias(ks[12], (DEPTH, D_GLA_K), 0.1),
        "gla_norm": gain(ks[13], (DEPTH, D_GLA_V)),
        "w_out": w(ks[14], (DEPTH, D_MIX, D_MODEL), D_MIX),
        "ffn2_norm": gain(ks[15], (DEPTH, D_MODEL)),
        "ffn2_w_in": w(ks[16], (DEPTH, D_MODEL, 2 * D_FF), D_MODEL),
        "ffn2_w_out": w(ks[17], (DEPTH, D_FF, D_MODEL), D_FF),
        "ple_norm": gain(ks[18], (DEPTH, D_MODEL)),
        "ple_w_gate": w(ks[19], (DEPTH, D_MODEL, D_MODEL), D_MODEL),
        "ple_w_proj": w(ks[20], (DEPTH, D_PLE, D_MODEL), D_PLE),
        "final_norm": gain(ks[21], (D_MODEL,)),
    }

def first_block(x, p, ffn1_norm, ffn1_w_in, ffn1_w_out, mix_norm, w_in, conv_w, conv_b,
              conv_ln_g, conv_ln_b, gate_w_up, gate_b, gla_norm, w_out, ffn2_norm,
              ffn2_w_in, ffn2_w_out, ple_norm, ple_w_gate, ple_w_proj, final_norm):
    h = x
    for i in range(DEPTH):
        h = h + 0.5 * _swiglu(_rmsnorm(h, ffn1_norm[i]), ffn1_w_in[i], ffn1_w_out[i])
        z = _rmsnorm(h, mix_norm[i]) @ w_in[i]
        conv_a, conv_gt, q, k, v, r, g_lr = jnp.split(z, SPLIT_POINTS, axis=-1)
        y_conv = _conv_module(conv_a, conv_gt, conv_w[i], conv_b[i], conv_ln_g[i], conv_ln_b[i])
        y_gla = _gla(q, k, v, r, g_lr, gate_w_up[i], gate_b[i], gla_norm[i])
        h = h + jnp.concatenate([y_conv, y_gla], axis=-1) @ w_out[i]
        h = h + 0.5 * _swiglu(_rmsnorm(h, ffn2_norm[i]), ffn2_w_in[i], ffn2_w_out[i])
        gate = jax.nn.sigmoid(_rmsnorm(h, ple_norm[i]) @ ple_w_gate[i])
        h = h + gate * (p[i] @ ple_w_proj[i])
    return _rmsnorm(h, final_norm)


DEPTH_2 = 2

N_MIXERS = 2
N_A_LAYERS = (DEPTH_2 + 1) // 2
N_B_LAYERS = DEPTH_2 // 2
DA_HEADS = 8
DA_HEAD_DIM = 64
DA_V_DIM = 2 * DA_HEAD_DIM
Q_BLOCK = 128
REL_BUCKETS = 32
REL_MAX_EXACT = REL_BUCKETS // 2
REL_MAX_DIST = 128
SGU_CHUNK = 128
SGU_WIDTH = D_MODEL
SGU_GROUPS = 8
SGU_GROUP_DIM = SGU_WIDTH // SGU_GROUPS
N_MOD = 9
NEG_INF = -1e30


def rms_norm(x, g):
    x32 = x.astype(jnp.float32)
    y = x32 * lax.rsqrt(jnp.mean(x32 * x32, axis=-1, keepdims=True) + EPS)
    return (y * g.astype(jnp.float32)).astype(x.dtype)

def layer_norm(x, g, b):
    x32 = x.astype(jnp.float32)
    mu = jnp.mean(x32, axis=-1, keepdims=True)
    xc = x32 - mu
    y = xc * lax.rsqrt(jnp.mean(xc * xc, axis=-1, keepdims=True) + EPS)
    return (y * g.astype(jnp.float32) + b.astype(jnp.float32)).astype(x.dtype)

def modulate(h, shift, scale):
    return h * (1.0 + scale[:, None, :]) + shift[:, None, :]

def swiglu(h, wg, wu, wd):
    return (jax.nn.silu(h @ wg) * (h @ wu)) @ wd

def t5_bucket(rel):
    n = jnp.maximum(rel, 0)
    nf = jnp.maximum(n, 1).astype(jnp.float32)
    large = REL_MAX_EXACT + (jnp.log(nf / REL_MAX_EXACT) / math.log(REL_MAX_DIST / REL_MAX_EXACT)
                             * (REL_BUCKETS - REL_MAX_EXACT)).astype(jnp.int32)
    large = jnp.minimum(large, REL_BUCKETS - 1)
    return jnp.where(n < REL_MAX_EXACT, n, large)

def diff_attention(h, w_qkv, q_g, k_g, lq1, lk1, lq2, lk2, subln_g, w_o, rel_bias, lambda_init):
    B, S, _ = h.shape
    q, k, v = jnp.split(h @ w_qkv, 3, axis=-1)
    q = rms_norm(q.reshape(B, S, DA_HEADS, 2, DA_HEAD_DIM), q_g)
    k = rms_norm(k.reshape(B, S, DA_HEADS, 2, DA_HEAD_DIM), k_g)
    v32 = v.reshape(B, S, DA_HEADS, DA_V_DIM).astype(jnp.float32)
    k32 = k.astype(jnp.float32)
    f32 = jnp.float32
    lam = (jnp.exp(jnp.sum(lq1.astype(f32) * lk1.astype(f32)))
           - jnp.exp(jnp.sum(lq2.astype(f32) * lk2.astype(f32))) + lambda_init)
    scale = 1.0 / math.sqrt(DA_HEAD_DIM)
    nb = S // Q_BLOCK
    qb = q.reshape(B, nb, Q_BLOCK, DA_HEADS, 2, DA_HEAD_DIM).transpose(1, 0, 2, 3, 4, 5)
    k_pos = jnp.arange(S, dtype=jnp.int32)
    table = rel_bias.astype(f32)

    def block(args):
        q_blk, bi = args
        q_pos = bi * Q_BLOCK + jnp.arange(Q_BLOCK, dtype=jnp.int32)
        rel = q_pos[:, None] - k_pos[None, :]
        bias = jnp.where((rel >= 0)[..., None], table[t5_bucket(rel)], NEG_INF)
        bias = bias.transpose(2, 0, 1)
        logits = jnp.einsum('bqhcd,bkhcd->bhcqk', q_blk.astype(f32), k32) * scale + bias[None, :, None]
        p = jax.nn.softmax(logits, axis=-1)
        attn = p[:, :, 0] - lam * p[:, :, 1]
        o = jnp.einsum('bhqk,bkhe->bqhe', attn, v32)
        o = rms_norm(o, subln_g) * (1.0 - lambda_init)
        return o.reshape(B, Q_BLOCK, DA_HEADS * DA_V_DIM).astype(h.dtype)

    out = lax.map(block, (qb, jnp.arange(nb, dtype=jnp.int32)))
    out = out.transpose(1, 0, 2, 3).reshape(B, S, DA_HEADS * DA_V_DIM)
    return out @ w_o

def spatial_gating(h, w_in, ln_g, ln_b, w_s, b_s, w_out):
    B, S, _ = h.shape
    z = jax.nn.gelu(h @ w_in, approximate=False)
    u, v = jnp.split(z, 2, axis=-1)
    v = layer_norm(v, ln_g, ln_b)
    nc = S // SGU_CHUNK
    v = v.reshape(B, nc, SGU_CHUNK, SGU_GROUPS, SGU_GROUP_DIM)
    causal = jnp.tril(jnp.ones((SGU_CHUNK, SGU_CHUNK), dtype=w_s.dtype))
    mixed = jnp.einsum('gts,bnsgc->bntgc', w_s * causal, v) + b_s.T[:, :, None]
    gated = u * mixed.reshape(B, S, SGU_WIDTH)
    return gated @ w_out

def _normal(k, shape, std):
    return jax.random.normal(k, shape, jnp.float32) * std

def second_inputs(seed: int = 0) -> dict:
    key = jax.random.key(seed)
    ks = jax.random.split(key, 32)
    D, F = D_MODEL, D_FF
    gain = lambda k, shape: 1.0 + _normal(k, shape, 0.1)
    return {
        'x': _normal(ks[0], (BATCH, SEQ, D), 1.0),
        'c': _normal(ks[1], (BATCH, D), 1.0),
        'rel_bias': _normal(ks[2], (REL_BUCKETS, DA_HEADS), 0.5),
        'ada_w': _normal(ks[3], (DEPTH_2, D, N_MOD * D), 0.5 * D ** -0.5),
        'ada_b': _normal(ks[4], (DEPTH_2, N_MOD * D), 0.02),
        'ln_ffn1': gain(ks[5], (DEPTH_2, D)),
        'ffn1_wg': _normal(ks[6], (DEPTH_2, D, F), D ** -0.5),
        'ffn1_wu': _normal(ks[7], (DEPTH_2, D, F), D ** -0.5),
        'ffn1_wd': _normal(ks[8], (DEPTH_2, F, D), F ** -0.5),
        'ln_mix': gain(ks[9], (DEPTH_2, D)),
        'ln_ffn2': gain(ks[10], (DEPTH_2, D)),
        'ffn2_wg': _normal(ks[11], (DEPTH_2, D, F), D ** -0.5),
        'ffn2_wu': _normal(ks[12], (DEPTH_2, D, F), D ** -0.5),
        'ffn2_wd': _normal(ks[13], (DEPTH_2, F, D), F ** -0.5),
        'ln_out': gain(ks[14], (DEPTH_2, D)),
        'attn_w_qkv': _normal(ks[15], (N_A_LAYERS, D, 3 * D), D ** -0.5),
        'attn_q_norm': gain(ks[16], (N_A_LAYERS, DA_HEAD_DIM)),
        'attn_k_norm': gain(ks[17], (N_A_LAYERS, DA_HEAD_DIM)),
        'attn_lq1': _normal(ks[18], (N_A_LAYERS, DA_HEAD_DIM), 0.1),
        'attn_lk1': _normal(ks[19], (N_A_LAYERS, DA_HEAD_DIM), 0.1),
        'attn_lq2': _normal(ks[20], (N_A_LAYERS, DA_HEAD_DIM), 0.1),
        'attn_lk2': _normal(ks[21], (N_A_LAYERS, DA_HEAD_DIM), 0.1),
        'attn_subln': gain(ks[22], (N_A_LAYERS, DA_V_DIM)),
        'attn_w_o': _normal(ks[23], (N_A_LAYERS, D, D), D ** -0.5),
        'sgu_w_in': _normal(ks[24], (N_B_LAYERS, D, 2 * SGU_WIDTH), D ** -0.5),
        'sgu_ln_g': gain(ks[25], (N_B_LAYERS, SGU_WIDTH)),
        'sgu_ln_b': _normal(ks[26], (N_B_LAYERS, SGU_WIDTH), 0.02),
        'sgu_w_s': _normal(ks[27], (N_B_LAYERS, SGU_GROUPS, SGU_CHUNK, SGU_CHUNK), SGU_CHUNK ** -0.5),
        'sgu_b_s': gain(ks[28], (N_B_LAYERS, SGU_GROUPS, SGU_CHUNK)),
        'sgu_w_out': _normal(ks[29], (N_B_LAYERS, SGU_WIDTH, D), SGU_WIDTH ** -0.5),
    }

def second_block(x, c, rel_bias, ada_w, ada_b, ln_ffn1, ffn1_wg, ffn1_wu, ffn1_wd, ln_mix,
              ln_ffn2, ffn2_wg, ffn2_wu, ffn2_wd, ln_out, attn_w_qkv, attn_q_norm, attn_k_norm,
              attn_lq1, attn_lk1, attn_lq2, attn_lk2, attn_subln, attn_w_o, sgu_w_in, sgu_ln_g,
              sgu_ln_b, sgu_w_s, sgu_b_s, sgu_w_out):
    c_act = jax.nn.silu(c)
    for i in range(DEPTH_2):
        mod = c_act @ ada_w[i] + ada_b[i]
        sh1, sc1, g1, sh2, sc2, g2, sh3, sc3, g3 = jnp.split(mod, N_MOD, axis=-1)
        h = modulate(rms_norm(x, ln_ffn1[i]), sh1, sc1)
        x = x + 0.5 * g1[:, None, :] * swiglu(h, ffn1_wg[i], ffn1_wu[i], ffn1_wd[i])
        h = modulate(rms_norm(x, ln_mix[i]), sh2, sc2)
        j = i // N_MIXERS
        if i % N_MIXERS == 0:
            lambda_init = 0.8 - 0.6 * math.exp(-0.3 * i)
            mix = diff_attention(h, attn_w_qkv[j], attn_q_norm[j], attn_k_norm[j], attn_lq1[j],
                                 attn_lk1[j], attn_lq2[j], attn_lk2[j], attn_subln[j], attn_w_o[j],
                                 rel_bias, lambda_init)
        else:
            mix = spatial_gating(h, sgu_w_in[j], sgu_ln_g[j], sgu_ln_b[j], sgu_w_s[j], sgu_b_s[j],
                                 sgu_w_out[j])
        x = x + g2[:, None, :] * mix
        h = modulate(rms_norm(x, ln_ffn2[i]), sh3, sc3)
        x = x + 0.5 * g3[:, None, :] * swiglu(h, ffn2_wg[i], ffn2_wu[i], ffn2_wd[i])
        x = rms_norm(x, ln_out[i])
    return x


def setup_inputs(seed=0):
    out = dict(first_inputs(seed))
    for name, value in second_inputs(seed + 1).items():
        if name != "x":
            out[name + "_2"] = value
    return out


def reference(
    x, p, ffn1_norm, ffn1_w_in, ffn1_w_out, mix_norm, w_in, conv_w, conv_b, conv_ln_g,
    conv_ln_b, gate_w_up, gate_b, gla_norm, w_out, ffn2_norm, ffn2_w_in, ffn2_w_out, ple_norm,
    ple_w_gate, ple_w_proj, final_norm, c_2, rel_bias_2, ada_w_2, ada_b_2, ln_ffn1_2, ffn1_wg_2,
    ffn1_wu_2, ffn1_wd_2, ln_mix_2, ln_ffn2_2, ffn2_wg_2, ffn2_wu_2, ffn2_wd_2, ln_out_2,
    attn_w_qkv_2, attn_q_norm_2, attn_k_norm_2, attn_lq1_2, attn_lk1_2, attn_lq2_2, attn_lk2_2,
    attn_subln_2, attn_w_o_2, sgu_w_in_2, sgu_ln_g_2, sgu_ln_b_2, sgu_w_s_2, sgu_b_s_2,
    sgu_w_out_2,
):
    x = first_block(
        x, p, ffn1_norm, ffn1_w_in, ffn1_w_out, mix_norm, w_in, conv_w, conv_b, conv_ln_g,
        conv_ln_b, gate_w_up, gate_b, gla_norm, w_out, ffn2_norm, ffn2_w_in, ffn2_w_out,
        ple_norm, ple_w_gate, ple_w_proj, final_norm,
    )
    return second_block(
        x, c_2, rel_bias_2, ada_w_2, ada_b_2, ln_ffn1_2, ffn1_wg_2, ffn1_wu_2, ffn1_wd_2,
        ln_mix_2, ln_ffn2_2, ffn2_wg_2, ffn2_wu_2, ffn2_wd_2, ln_out_2, attn_w_qkv_2,
        attn_q_norm_2, attn_k_norm_2, attn_lq1_2, attn_lk1_2, attn_lq2_2, attn_lk2_2,
        attn_subln_2, attn_w_o_2, sgu_w_in_2, sgu_ln_g_2, sgu_ln_b_2, sgu_w_s_2, sgu_b_s_2,
        sgu_w_out_2,
    )


_drawn_inputs = setup_inputs


def setup_inputs(seed=0):
    import zlib

    import numpy as np

    out = dict(_drawn_inputs(seed))
    spreads = {}
    factors = {'conv_b': 3.447,
     'conv_ln_g': 2.671,
     'conv_ln_b': 7.12,
     'gate_b': 4.303,
     'gla_norm': 3.338,
     'ffn2_norm': 3.454,
     'ple_norm': 7.244,
     'ln_ffn1_2': 2.74,
     'ln_ffn2_2': 2.715,
     'attn_q_norm_2': 4.396,
     'attn_k_norm_2': 4.265,
     'attn_lq1_2': 64.0,
     'attn_lk1_2': 4.642,
     'attn_lq2_2': 48.104,
     'attn_subln_2': 12.989,
     'sgu_ln_g_2': 3.65,
     'sgu_ln_b_2': 25.606,
     'sgu_b_s_2': 2.712,
     'attn_lk2_2': 8.0}
    for name, (base, spread) in spreads.items():
        noise = np.random.default_rng([zlib.crc32(name.encode()), seed]).standard_normal(out[name].shape)
        drawn = base * np.exp(spread * noise) if base else spread * noise
        out[name] = __import__('jax').numpy.asarray(drawn.astype(out[name].dtype))
    for name, factor in factors.items():
        out[name] = (out[name] * factor).astype(out[name].dtype)
    return out
```

```python
from contextlib import ExitStack

import numpy as np

import concourse.bass as bass
from concourse import mybir

ALU = mybir.AluOpType
ACT = mybir.ActivationFunctionType
F32 = mybir.dt.float32
F32R = mybir.dt.float32r
I32 = mybir.dt.int32
AX_X = mybir.AxisListType.X

P = 128
T = 256
D = 1024
KT = D // P
F = 2816
NC = 256
STEPS = F // NC
SLOTS = 3
CH = KT * NC
EPS = 1e-6
CONV = 31
CT = 4
HG = 4
CHUNK = 64
HA = 8
NB = 32
LAMBDA_INIT = 0.2
FLT_MAX = float(np.finfo(np.float32).max)
TINY = 1e-36
ADA_W = 512
ADA_BLOCKS = 9 * D // ADA_W
LOOPED = STEPS - 2
assert ADA_BLOCKS == 2 * LOOPED and CH == 2 * D

STAGES = [("ffn", 33), ("mix", 14), ("ffn", 33), ("ple", 5), ("renorm", 0),
          ("ffn", 33), ("attn", 16), ("ffn", 33), ("renorm", 0),
          ("ffn", 33), ("sgu", 12), ("ffn", 33), ("renorm", 0)]
BASE = [sum(c for _, c in STAGES[:n]) for n in range(len(STAGES))]
TOTAL = sum(c for _, c in STAGES)
SPLIT_NO = [sum(k != "renorm" for k, _ in STAGES[:n]) for n in range(len(STAGES))]
FFN_NO = [sum(k == "ffn" for k, _ in STAGES[:n]) for n in range(len(STAGES))]

COLS = {}
_at = 0
for _name, _n in [("ffn1_norm", 8), ("mix_norm", 8), ("ffn2_norm", 8), ("ple_norm", 8), ("final_norm", 8),
                  ("ln_ffn1_2", 16), ("ln_mix_2", 16), ("ln_ffn2_2", 16), ("ln_out_2", 16),
                  ("conv_b", 4), ("conv_ln_g", 4), ("conv_ln_b", 4), ("gla_norm", 4), ("conv_w", 4 * CONV),
                  ("attn_q_norm_2", 1), ("attn_k_norm_2", 1), ("attn_subln_2", 1), ("c_2", 8),
                  ("ada_b_2", 144)]:
    COLS[_name] = (_at, _n)
    _at += _n
NCOLS = _at
SKEW = 384


def two_blocks(nc, a, out):
    with ExitStack() as ctx:
        def sb(name, shape, dt=F32):
            return ctx.enter_context(nc.sbuf_tensor(name, shape, dt))

        def sem(name):
            return ctx.enter_context(nc.semaphore(name))

        raw = sb("raw", [P, SLOTS, CH])
        w_hi = sb("w_hi", [P, SLOTS, CH], F32R)
        w_lo = sb("w_lo", [P, SLOTS, CH], F32R)
        x = sb("x_res", [P, KT, T])
        xs_hi = sb("xs_hi", [P, KT, T], F32R)
        xs_lo = sb("xs_lo", [P, KT, T], F32R)
        cs_hi = sb("cs_hi", [P, KT, T], F32R)
        cs_lo = sb("cs_lo", [P, KT, T], F32R)
        xn = sb("xn", [P, KT, T])
        ub = sb("ub", [P, KT, T])
        ada = sb("ada", [P, 2, 4 * ADA_W])
        ada_acc = sb("ada_acc", [P, ADA_W])
        silu_g = sb("silu_g", [P, 2 * T])
        gu = sb("gu", [P, 2 * T])
        gu_hi = sb("gu_hi", [P, 2 * T], F32R)
        gu_lo = sb("gu_lo", [P, 2 * T], F32R)
        rt = sb("rt", [P, 2 * T])
        rstd = sb("rstd", [P, 2 * T])
        cols = sb("cols_sb", [P, NCOLS])
        consts = sb("consts_sb", [P, 6, P])
        tri, low_mask, up_mask, ident, causal, pair_ones = (consts[:, i, :] for i in range(6))
        ones_d = sb("ones_d", [P, P])
        ones_c = sb("ones_c", [P, P])
        ones_v = sb("ones_v", [P, P])
        ones_1 = sb("ones_1", [P, P])
        eps_col = sb("eps_col", [P, 1])
        one_col = sb("one_col", [P, 1])
        zero_col = sb("zero_col", [P, 1])
        c_act = sb("c_act", [P, KT])
        mod = sb("mod", [P, 2, 72])
        a_col = sb("a_col", [P, 2, 3 * KT])
        half_g = sb("half_g", [P, 2, 2 * KT])
        nlam = sb("nlam", [P, 1])
        lam_size = sb("lam_size", [P, 1])
        lam_r = sb("lam_r", [P, 1])
        lam_coef = sb("lam_coef", [P, 4])
        eps_sub = sb("eps_sub", [P, 1])
        ms_limit = sb("ms_limit", [P, 1])
        lam_in = sb("lam_in", [64, 8])
        lam_e = sb("lam_e", [P, 2])
        sub_g = sb("sub_g", [P, 1])
        ARENA = 9400
        arena = sb("arena", [P, ARENA])
        top = [0]

        def carve(n, rows=P):
            top[0] += n
            assert top[0] <= ARENA, top[0]
            return arena[0:rows, top[0] - n:top[0]]

        glu = carve(CT * (T + CONV - 1)).rearrange("p (c t) -> p c t", c=CT)
        conv_y = carve(CT * T).rearrange("p (c t) -> p c t", c=CT)
        q_s, k_s, log_a, e_pos, e_neg, k_exp = (carve(2 * T) for _ in range(6))
        ke_t = carve(2 * T).rearrange("p (a n) -> p a n", a=2)
        score = [carve(2 * T).rearrange("p (n t) -> p n t", n=4) for _ in range(2)]
        state = carve(3 * 2 * P).rearrange("p (c h v) -> p c h v", c=3, h=2)
        v_tok = carve(4 * T).rearrange("p (m a n) -> p m a n", m=2, a=2)
        glr = carve(T, 32)
        wup = carve(T, 32)
        w_glr = carve(KT * 16).rearrange("p (k n) -> p k n", k=KT)
        cum_end = carve(8)
        decay = carve(8)
        ada_flat = ada[:, :, :].rearrange("p a n -> p (a n)")
        q_dec, k_neg, q_neg, k_pos, k_end = (ada_flat[:, i * 2 * T:(i + 1) * 2 * T] for i in range(5))
        silu_r = ada_flat[:, 10 * T:14 * T].rearrange("p (c t) -> p c t", c=4)
        top[0] = 0
        bias_t = carve(HA * SKEW).rearrange("p (h j) -> p h j", h=HA)
        q_raw, k_raw, qk_sq, q_n, k_n = (carve(2 * T) for _ in range(5))
        va = carve(2 * T).rearrange("p (a n) -> p a n", a=2)
        logit = carve(2 * SKEW).rearrange("p (c j) -> p c j", c=2)
        attn = carve(SKEW)
        attn_t = carve(SKEW)
        peak, total, recip, coef = (carve(4) for _ in range(4))
        table = carve(HA, NB + 1)
        one_hot = carve(SKEW, NB + 1)
        table_b = carve(P, NB + 1)
        top[0] = 0
        ln_rows = carve(2 * D).rearrange("p (a n) -> p a n", a=2)
        w_mix = carve(KT * P).rearrange("p (g t) -> p g t", g=KT)
        v_g = carve(2 * D).rearrange("p (a n) -> p a n", a=2)
        b_mix = carve(KT * P, 1).rearrange("p (g t) -> p g t", g=KT)
        v_sum, v_mean, v_var, v_rt, v_rstd = (carve(2) for _ in range(5))

        bank = [ctx.enter_context(nc.psum_tensor(f"bank{i}", [P, 2 * T], F32)) for i in range(8)]
        GATE, UP, MISC, STAT = 4, 5, 6, 7
        skew = nc.dram_tensor("skew_scratch", [HA, P, SKEW], F32).ap()

        raw_in = [sem(f"raw_in{i}") for i in range(SLOTS)]
        hi_ready, lo_ready, chunks_done = sem("hi_ready"), sem("lo_ready"), sem("chunks_done")
        x_in, x_ready, sq_ready, ss_ready = sem("x_in"), sem("x_ready"), sem("sq_ready"), sem("ss_ready")
        rt_ready, rstd_ready, t_ready = sem("rt_ready"), sem("rstd_ready"), sem("t_ready")
        xhi_ready, xs_ready = sem("xhi_ready"), sem("xs_ready")
        silu_done, gu_ready, guhi_ready, gulo_ready = (sem(s) for s in ("silu_done", "gu_ready", "guhi_ready", "gulo_ready"))
        bank_done = sem("bank_done")
        ada_in = [sem("ada_in0"), sem("ada_in1")]
        ada_step, ada_summed, ada_stored = sem("ada_step"), sem("ada_summed"), sem("ada_stored")
        cs_t, cs_hi_ready, cs_ready = sem("cs_t"), sem("cs_hi_ready"), sem("cs_ready")
        consts_in, memsets, dve_chain = sem("consts_in"), sem("memsets"), sem("dve_chain")
        act_chain = sem("act_chain")
        out_done = sem("out_done")
        S = {}

        def ev(name):
            if name not in S:
                S[name] = sem(name)
            return S[name]

        block = ctx.enter_context(nc.Block())

        def col(name, i=0):
            at = COLS[name][0] + i
            return cols[:, at:at + 1]

        def modc(layer, m, k, n=1):
            return mod[:, layer, 8 * m + k:8 * m + k + n]

        def norm_cols(n):
            plain = {0: "ffn1_norm", 1: "mix_norm", 2: "ffn2_norm", 3: "ple_norm", 4: "final_norm"}
            if n in plain:
                return (lambda k: col(plain[n], k)), None
            if n in (8, 12):
                return (lambda k: col("ln_out_2", 8 * (n // 12) + k)), None
            layer, j = (0, n - 5) if n < 8 else (1, n - 9)
            return (lambda k: a_col[:, layer, 8 * j + k:8 * j + k + 1]), (lambda k: modc(layer, 3 * j, k))

        def lin(slot, w):
            return w[:, slot, :].rearrange("p (k n) -> p k n", k=KT)

        def tail(slot, w):
            return w[:, slot, :].rearrange("p (j n) -> p j n", j=2)

        MIX_COLS = [0, 512, 256, 768, 1024, 1280, 1536, 1792, 2048, 2304]
        L = 2

        @block.sync
        def _(sp):
            def load(c, src, n=None):
                s = n if n is not None else c % SLOTS
                if n is not None or c >= SLOTS:
                    sp.wait_ge(hi_ready, c - SLOTS + 1)
                    sp.wait_ge(lo_ready, c - SLOTS + 1)
                sp.dma_start(raw[:, s, :].rearrange("p (k n) -> p k n", k=src.shape[1]), src)\
                    .then_inc(raw_in[s], 16)

            def over_k(w, at):
                return w[:, bass.ds(at, NC)].rearrange("(k p) n -> p k n", p=P)

            def over_f(w, at):
                return w[bass.ds(at, NC), :].rearrange("(j p) n -> p j n", p=P)

            def load_ada(layer, block_no, after):
                for half in range(2):
                    if after is not None:
                        sp.wait_ge(ada_step, after + 4 * half + 4)
                    src = a["ada_w_2"][layer, half * 512:(half + 1) * 512, bass.ds(block_no * ADA_W, ADA_W)]
                    sp.dma_start(ada[:, half, :].rearrange("p (k n) -> p k n", k=4),
                                 src.rearrange("(k p) n -> p k n", p=P)).then_inc(ada_in[half], 16)

            def ffn_weights(n):
                f = FFN_NO[n]
                if f < 2:
                    w_in, w_down = a[f"ffn{f + 1}_w_in"][0], a[f"ffn{f + 1}_w_out"][0]
                    return w_in[:, 0:F], w_in[:, F:2 * F], w_down
                layer, j = (f - 2) // 2, f % 2 + 1
                return tuple(a[f"ffn{j}_{w}_2"][layer] for w in ("wg", "wu", "wd"))

            def ffn(n):
                gate, up, down = ffn_weights(n)
                f, c0 = FFN_NO[n], BASE[n]
                load(c0, over_k(gate, 0))
                load(c0 + 1, over_k(up, 0))
                load(c0 + 2, over_k(gate, NC))
                load(c0 + 3, over_k(up, NC))
                load(c0 + 4, over_f(down, 0))
                cl = c0 + 5
                with_ada = f < 4
                layer, first = f // 2, (f % 2) * LOOPED

                def step(i, ada_i):
                    load(cl + 3 * i, over_k(gate, (i + 2) * NC), cl % SLOTS)
                    load(cl + 3 * i + 1, over_k(up, (i + 2) * NC), (cl + 1) % SLOTS)
                    if isinstance(ada_i, int) and f == 0:
                        load_ada(layer, first, None)
                    elif ada_i is not None:
                        load_ada(layer, ada_i + first, (ada_i + f * LOOPED - 1) * 8)
                    load(cl + 3 * i + 2, over_f(down, (i + 1) * NC), (cl + 2) % SLOTS)

                step(0, None)
                if with_ada:
                    if f > 0:
                        sp.wait_ge(x_ready, 8 * n)
                    step(1, 0)
                    with sp.Fori(2, LOOPED) as i:
                        step(i, i - 1)
                    load_ada(layer, LOOPED - 1 + first, (LOOPED - 2 + f * LOOPED) * 8)
                else:
                    with sp.Fori(1, LOOPED) as i:
                        step(i, None)
                load(c0 + 32, over_f(down, (STEPS - 1) * NC))

            sp.dma_start(x[:, :, :], a["x"]).then_inc(x_in, 16)
            sp.dma_start(cols[:, :], a["cols"]).then_inc(consts_in, 16)
            sp.dma_start(consts[:, :, :], a["consts"]).then_inc(consts_in, 16)
            for n, (kind, _) in enumerate(STAGES):
                c0 = BASE[n]
                if kind == "ffn":
                    ffn(n)
                elif kind == "mix":
                    for j, at in enumerate(MIX_COLS):
                        load(c0 + j, over_k(a["w_in"][0], at))
                    for j in range(4):
                        load(c0 + 10 + j, over_k(a["w_out"][0], j * NC))
                elif kind == "ple":
                    load(c0, over_f(a["ple_w_proj"][0], 0))
                    for j in range(4):
                        load(c0 + 1 + j, over_k(a["ple_w_gate"][0], j * NC))
                elif kind == "attn":
                    w = a["attn_w_qkv_2"][0]
                    for i in range(4):
                        for part in range(3):
                            load(c0 + 3 * i + part, over_k(w, part * D + i * NC))
                    for j in range(4):
                        load(c0 + 12 + j, over_k(a["attn_w_o_2"][0], j * NC))
                elif kind == "sgu":
                    w = a["sgu_w_in_2"][0]
                    for j in range(4):
                        load(c0 + j, over_k(w, D + j * NC))
                    for j in range(4):
                        load(c0 + 4 + j, over_k(w, j * NC))
                    for j in range(4):
                        load(c0 + 8 + j, over_k(a["sgu_w_out_2"][0], j * NC))
            sp.wait_ge(x_ready, 8 * len(STAGES))
            sp.dma_start(out, x[:, :, :]).then_inc(out_done, 16)
            sp.wait_ge(out_done, 16)

        @block.gpsimd
        def _(pool):
            pool.memset(eps_col[:, :], EPS).then_inc(memsets, 1)
            pool.memset(one_col[:, :], 1.0).then_inc(memsets, 1)
            pool.memset(ones_d[:, :], 1.0 / D).then_inc(memsets, 1)
            pool.memset(ones_c[:, :], 1.0 / (CT * P)).then_inc(memsets, 1)
            pool.memset(ones_v[:, :], 1.0 / P).then_inc(memsets, 1)
            pool.memset(ones_1[:, :], 1.0).then_inc(memsets, 1)
            pool.memset(zero_col[:, :], 0.0).then_inc(memsets, 1)
            pool.wait_ge(memsets, 7)
            pool.memset(table[NB:NB + 1, :], -1e30).then_inc(memsets, 1)
            pool.dma_start(table[0:NB, :], a["rel_bias_2"]).then_inc(ev("table_in"), 16)
            pool.dma_start(one_hot, a["one_hot"]).then_inc(ev("table_in"), 16)
            pool.dma_start(lam_in[:, 0:4], a["lam"]).then_inc(ev("lam_in"), 16)
            pool.wait_ge(ev("skew_copied"), HA)
            pool.dma_start(skew.rearrange("h p j -> p h j"), bias_t).then_inc(ev("skew_out"), 16)
            pool.wait_ge(ev("skew_out"), 16)
            if len(STAGES) > 1:
                pool.memset(glu[:, :, 0:CONV - 1], 0.0).then_inc(ev("glu_pad"), 1)
                pool.wait_ge(ev("glu_pad"), 1)
                pool.memset(glr, 1.0).then_inc(ev("glr_ones"), 1)
                pool.wait_ge(ev("glr_ones"), 1)
                pool.dma_start(w_glr, a["w_in"][0][:, 2560:2576].rearrange("(k p) n -> p k n", p=P))\
                    .then_inc(ev("gate_w_in"), 16)
                pool.dma_start(wup[0:16, :], a["gate_w_up"][0]).then_inc(ev("gate_w_in"), 16)
                pool.dma_start(wup[16:17, :], a["gate_b"]).then_inc(ev("gate_w_in"), 16)
                for par in range(2):
                    pool.memset(score[par], 0.0).then_inc(ev("score_zero"), 1)
                    pool.wait_ge(ev("score_zero"), par + 1)
            if len(STAGES) > 3:
                pool.wait_ge(x_ready, 8 * 2)
                pool.dma_start(ub[:, 0:2, :], a["p"]).then_inc(ev("p_in"), 16)
            if len(STAGES) > 6:
                pool.wait_ge(x_ready, 8 * 2)
                skewed = skew.rearrange("h p j -> (h p j)")
                for lo, n, at in ((SKEW - T, T, 0), (0, P, P)):
                    src = bass.AP(skewed.tensor, P - 1 + at, [[SKEW - 1, P], [P * SKEW, HA], [1, n]])
                    pool.dma_start(bias_t[:, :, (P if n == T else 0):(P if n == T else 0) + n], src)\
                        .then_inc(ev("bias_in"), 16)
            if len(STAGES) > 10:
                pool.wait_ge(x_ready, 8 * 7)
                pool.dma_start(ln_rows[:, 0, :], a["sgu_ln_g_2"][0:1, :].to_broadcast([P, D])).then_inc(ev("sgu_in"), 16)
                pool.dma_start(ln_rows[:, 1, :], a["sgu_ln_b_2"][0:1, :].to_broadcast([P, D])).then_inc(ev("sgu_in"), 16)
                pool.dma_start(w_mix, a["w_mix"]).then_inc(ev("sgu_in"), 16)
                pool.dma_start(b_mix, a["sgu_b_s_2"]).then_inc(ev("sgu_in"), 16)

        @block.scalar
        def _(act):
            def split(c, s=None):
                looped = s is not None
                if not looped and c >= TOTAL:
                    return
                s = c % SLOTS if s is None else s
                if looped:
                    act.wait_ge(raw_in[s], (c[0] // SLOTS + 1) * 16 + c[1] * 16)
                    act.wait_ge(chunks_done, c[0] - SLOTS + 1 + c[1] * 3)
                else:
                    act.wait_ge(raw_in[s], 16 * (c // SLOTS + 1))
                    if c >= SLOTS:
                        act.wait_ge(chunks_done, c - SLOTS + 1)
                act.activation(w_hi[:, s, :], raw[:, s, :], ACT.Copy).then_inc(hi_ready, 1)

            def norm(n, before_sq=None):
                kind = STAGES[n][0]
                for k in range(KT):
                    if n == 0:
                        act.wait_ge(x_in, 16)
                    else:
                        act.wait_ge(x_ready, 8 * (n - 1) + k + 1)
                    act.activation(xn[:, k, :], x[:, k, :], ACT.Square).then_inc(sq_ready, 1)
                act.wait_ge(ss_ready, n + 1)
                act.activation(rt[:, 0:T], bank[STAT][:, 0:T], ACT.Sqrt, bias=eps_col[:, :]).then_inc(rt_ready, 1)
                if kind == "renorm":
                    return
                shift = norm_cols(n)[1]
                for k in range(KT):
                    act.wait_ge(t_ready, 8 * SPLIT_NO[n] + k + 1)
                    if shift is None:
                        act.activation(xs_hi[:, k, :], xn[:, k, :], ACT.Copy).then_inc(xhi_ready, 1)
                    else:
                        act.activation(xs_hi[:, k, :], xn[:, k, :], ACT.Identity, bias=shift(k)).then_inc(xhi_ready, 1)

            def ffn(n):
                f, c0 = FFN_NO[n], BASE[n]
                s0 = STEPS * f

                def silu(s, c):
                    act.wait_ge(chunks_done, c + 1)
                    act.activation(silu_g[:, :], bank[GATE][:, :], ACT.Silu).then_inc(silu_done, 1)

                def gu_high(s, c):
                    act.wait_ge(gu_ready, s0 + s + 1)
                    if c is not None:
                        act.wait_ge(chunks_done, c + 1)
                    act.activation(gu_hi[:, :], gu[:, :], ACT.Copy).then_inc(guhi_ready, 1)

                split(c0 + 2)
                silu(0, c0)
                split(c0 + 3)
                gu_high(0, None)
                split(c0 + 4)
                silu(1, c0 + 2)
                split(c0 + 5)
                cl = c0 + 5
                with act.Fori(0, LOOPED) as i:
                    split((cl + 1, i), (cl + 1) % SLOTS)
                    gu_high(i + 1, cl + 3 * i - 1)
                    split((cl + 2, i), (cl + 2) % SLOTS)
                    silu(i + 2, cl + 3 * i)
                    split((cl + 3, i), (cl + 3) % SLOTS)
                split(c0 + 33)
                gu_high(STEPS - 1, c0 + 31)
                split(c0 + 34)

            def mix(n):
                c = BASE[n]
                split(c + 2)
                split(c + 3)
                for pair, s in ((0, c + 4), (1, c + 6)):
                    act.wait_ge(chunks_done, c + 2 * pair + 2)
                    if pair:
                        act.wait_ge(ev("glu_done"), 1)
                    act.activation(silu_g[:, :], bank[1 + 2 * pair][:, :], ACT.Sigmoid).then_inc(ev("conv_sig"), 1)
                    split(s)
                    if not pair:
                        split(c + 5)
                act.wait_ge(chunks_done, c + 5)
                act.wait_ge(ev("skew_out"), 16)
                act.activation(q_s, bank[4][:, :], ACT.Copy, scale=HEAD_SCALE).then_inc(ev("qk_copied"), 1)
                split(c + 7)
                act.wait_ge(chunks_done, c + 6)
                act.activation(k_s, bank[5][:, :], ACT.Copy).then_inc(ev("qk_copied"), 1)
                act.wait_ge(ev("glr_done"), 1)
                act.wait_ge(ev("glr_ones"), 1)
                act.activation(glr[0:16, :], bank[MISC][0:16, 0:T], ACT.Copy).then_inc(ev("glr_copied"), 1)
                split(c + 8)
                act.wait_ge(chunks_done, c + 7)
                act.activation(v_tok[:, 0, :, :], bank[0][:, :].rearrange("p (a n) -> p a n", a=2), ACT.Copy)\
                    .then_inc(ev("v_copied"), 1)
                act.wait_ge(ev("z_done"), 1)
                act.activation(e_pos, bank[STAT][:, :], ACT.Abs).then_inc(ev("la_act"), 1)
                act.wait_ge(ev("la_act"), 1)
                act.activation(e_neg, e_pos, ACT.Exp, scale=-1.0).then_inc(ev("la_act"), 1)
                act.wait_ge(ev("la_act"), 2)
                act.activation(e_pos, e_neg, ACT.Ln, bias=one_col[:, :]).then_inc(ev("la_act"), 1)
                split(c + 9)
                act.wait_ge(chunks_done, c + 8)
                act.activation(v_tok[:, 1, :, :], bank[1][:, :].rearrange("p (a n) -> p a n", a=2), ACT.Copy)\
                    .then_inc(ev("v_copied"), 1)
                act.wait_ge(ev("cum_done"), 1)
                act.activation(e_pos, bank[MISC][:, :], ACT.Exp).then_inc(ev("e_done"), 1)
                act.activation(e_neg, bank[MISC][:, :], ACT.Exp, scale=-1.0).then_inc(ev("e_done"), 1)
                split(c + 10)
                act.wait_ge(ev("cum_end"), 1)
                for i in range(8):
                    act.activation(k_exp[:, i * CHUNK:(i + 1) * CHUNK], bank[MISC][:, i * CHUNK:(i + 1) * CHUNK],
                                   ACT.Exp, scale=-1.0, bias=cum_end[:, i:i + 1]).then_inc(ev("k_exp"), 1)
                act.activation(decay, cum_end, ACT.Exp).then_inc(ev("decay"), 1)
                for m in range(2):
                    act.wait_ge(chunks_done, c + 9 + m)
                    act.activation(silu_r[:, 2 * m:2 * m + 2, :], bank[2 + m][:, :].rearrange("p (a n) -> p a n", a=2),
                                   ACT.Silu).then_inc(ev("silu_r"), 1)
                    split(c + 11 + m)
                act.wait_ge(ev("ke_turned"), 1)
                act.activation(ke_t, bank[STAT][:, :].rearrange("p (a n) -> p a n", a=2), ACT.Copy)\
                    .then_inc(ev("ke_copied"), 1)
                for par in range(2):
                    act.wait_ge(ev("o_done"), par + 1)
                    act.activation(ub[:, 4 + 2 * par:6 + 2 * par, :], bank[6 + par][:, :].rearrange("p (a n) -> p a n", a=2),
                                   ACT.Square).then_inc(ev("o_sq"), 1)
                for par in range(2):
                    act.wait_ge(ev("o_ms"), par + 1)
                    act.activation(silu_g[:, :] if par else rt[:, :], bank[4 + par][:, :], ACT.Sqrt, bias=eps_col[:, :])\
                        .then_inc(ev("o_rt"), 1)
                for h in range(HG):
                    act.wait_ge(cs_t, h + 1)
                    act.activation(cs_hi[:, 4 + h, :], xn[:, 4 + h, :], ACT.Copy).then_inc(cs_hi_ready, 1)
                act.wait_ge(ev("ln_centred"), 1)
                act.activation(conv_y, ub[:, 0:4, :], ACT.Square).then_inc(ev("ln_sq"), 1)
                act.wait_ge(ev("ln_var"), 1)
                act.activation(rt[:, 0:T], bank[1][:, 0:T], ACT.Sqrt, bias=eps_col[:, :]).then_inc(ev("ln_rt"), 1)
                for k in range(CT):
                    act.wait_ge(ev("ln_t"), k + 1)
                    act.activation(xn[:, k, :], conv_y[:, k, :], ACT.Silu, scale=col("conv_ln_g", k),
                                   bias=col("conv_ln_b", k)).then_inc(ev("ln_silu"), 1)
                for k in range(CT):
                    act.wait_ge(ev("ln_silu"), k + 1)
                    act.activation(cs_hi[:, k, :], xn[:, k, :], ACT.Copy).then_inc(cs_hi_ready, 1)
                for j in range(4):
                    if j >= 1:
                        split(c + 12 + j)

            def ple(n):
                c = BASE[n]
                act.wait_ge(ev("p_in"), 16)
                act.activation(cs_hi[:, 0:2, :], ub[:, 0:2, :], ACT.Copy).then_inc(ev("p_hi"), 1)
                norm(n)
                split(c + 2)
                split(c + 3)
                for j in range(4):
                    act.wait_ge(chunks_done, c + 2 + j)
                    if j:
                        act.wait_ge(ev("ple_mul"), j)
                    act.activation(silu_g[:, :], bank[4 + j % 2][:, :], ACT.Sigmoid).then_inc(ev("ple_sig"), 1)
                    if j < 3:
                        split(c + 4 + j)

            def attention(n):
                c = BASE[n]

                def heads(i, j, ahead):
                    e = 2 * i + j
                    for m in range(4):
                        comp, part = m % 2, m // 2
                        act.wait_ge(ev("peak"), e + 1)
                        seg = logit[:, comp, (P if part else 0):(SKEW if part else P)]
                        act.activation(seg, seg, ACT.Exp, bias=peak[:, m:m + 1],
                                       accum_out=total[:, m:m + 1]).then_inc(ev("exp"), 1)

                def turned(i, j):
                    e = 2 * i + j
                    act.wait_ge(ev("turned"), e + 1)
                    act.activation(attn_t, bank[MISC][:, 0:SKEW], ACT.Copy).then_inc(ev("turned_copied"), 1)

                def outs(i):
                    act.wait_ge(ev("pair_done"), i + 1)
                    act.activation(xn[:, bass.ds(2 * i, 2), :] , bank[7][:, :].rearrange("p (a n) -> p a n", a=2),
                                   ACT.Copy).then_inc(ev("o_copied"), 1)

                def qk_in(i, which):
                    act.wait_ge(chunks_done, c + 3 * i + which + 1)
                    if which:
                        act.wait_ge(ev("qk_norm_ms"), 2 * i + 1)
                    act.activation((q_raw, k_raw)[which], bank[which][:, :], ACT.Copy).then_inc(ev("qk_raw"), 1)
                    act.activation(qk_sq, bank[which][:, :], ACT.Square).then_inc(ev("qk_sq"), 1)

                def qk_root(i, which):
                    act.wait_ge(ev("qk_norm_ms"), 2 * i + which + 1)
                    if which or not isinstance(i, int):
                        act.wait_ge(ev("qk_rstd"), 2 * i + which)
                    act.activation(rt[:, :], bank[3][:, :], ACT.Sqrt, bias=eps_col[:, :]).then_inc(ev("qk_rt"), 1)

                def values(i):
                    act.wait_ge(chunks_done, c + 3 * i + 3)
                    act.activation(va, bank[2][:, :].rearrange("p (a n) -> p a n", a=2), ACT.Copy)\
                        .then_inc(ev("va"), 1)

                def pair(i, c_at, before):
                    def sp_(m):
                        if isinstance(i, int):
                            split(c + 3 * i + m)
                        else:
                            split((c + 3 + m, i - 1), (c + 3 + m) % SLOTS)
                    sp_(2)
                    if before:
                        heads(i - 1, 0, None)
                    qk_in(i, 0)
                    sp_(3)
                    if before:
                        turned(i - 1, 0)
                        heads(i - 1, 1, None)
                    qk_root(i, 0)
                    qk_in(i, 1)
                    sp_(4)
                    if before:
                        turned(i - 1, 1)
                        outs(i - 1)
                    qk_root(i, 1)
                    values(i)

                pair(0, c, False)
                with act.Fori(1, 4) as i:
                    pair(i, None, True)
                split(c + 14)
                heads(3, 0, None)
                turned(3, 0)
                heads(3, 1, None)
                turned(3, 1)
                outs(3)
                for j in range(4):
                    act.wait_ge(ev("o_copied"), 4)
                    act.activation(ub[:, 2 * j:2 * j + 2, :], xn[:, 2 * j:2 * j + 2, :], ACT.Square)\
                        .then_inc(ev("sub_sq"), 1)
                for j in range(4):
                    act.wait_ge(ev("sub_ms"), j + 1)
                    if j:
                        act.wait_ge(ev("sub_rstd"), j)
                    act.activation(rt[:, :], bank[j][:, :], ACT.Sqrt, bias=eps_sub[:, :]).then_inc(ev("sub_rt"), 1)
                for k in range(KT):
                    act.wait_ge(cs_t, 4 + k + 1)
                    act.activation(cs_hi[:, k, :], ub[:, k, :], ACT.Copy).then_inc(cs_hi_ready, 1)
                split(c + 15)
                split(c + 16)
                split(c + 17)

            def gating(n):
                c = BASE[n]
                split(c + 2)
                for j in range(4):
                    if j:
                        split(c + 2 + j)
                    act.wait_ge(chunks_done, c + j + 1)
                    act.activation(v_g[:, :, j * NC:(j + 1) * NC], bank[j][:, :].rearrange("p (a n) -> p a n", a=2),
                                   ACT.Gelu).then_inc(ev("v_gelu"), 1)
                split(c + 6)
                for j in range(4):
                    act.wait_ge(chunks_done, c + 5 + j)
                    act.activation(ub[:, 2 * j:2 * j + 2, :], bank[4 + j % 2][:, :].rearrange("p (a n) -> p a n", a=2),
                                   ACT.Gelu).then_inc(ev("u_gelu"), 1)
                    if j == 1:
                        for t in range(2):
                            act.wait_ge(ev("v_centred"), 2)
                            act.activation(xn[:, 0:4, :] if t == 0 else xn[:, 4:8, :],
                                           v_g[:, t, :].rearrange("p (a n) -> p a n", a=4), ACT.Square,
                                           accum_out=v_var[:, t:t + 1]).then_inc(ev("v_sq"), 1)
                        act.wait_ge(ev("v_sq"), 2)
                        act.activation(v_rt, v_var, ACT.Sqrt, scale=1.0 / D, bias=eps_col[:, :]).then_inc(ev("v_rt"), 1)
                    if j < 3:
                        split(c + 7 + j)
                split(c + 10)
                for k in range(KT):
                    act.wait_ge(cs_t, 12 + k + 1)
                    act.activation(cs_hi[:, k, :], xn[:, k, :], ACT.Copy).then_inc(cs_hi_ready, 1)
                split(c + 11)
                split(c + 12)
                split(c + 13)

            act.wait_ge(memsets, 8)
            act.wait_ge(consts_in, 32)
            act.activation(c_act[:, :], cols[:, COLS["c_2"][0]:COLS["c_2"][0] + KT], ACT.Silu).then_inc(ev("c_act"), 1)
            act.wait_ge(ev("lam_sum"), 1)
            act.activation(lam_e[:, :], bank[STAT][:, 0:2], ACT.Exp).then_inc(ev("lam_exp"), 1)
            split(0)
            split(1)
            norm(0)
            for n, (kind, _) in enumerate(STAGES):
                if n and kind != "ple":
                    norm(n)
                {"ffn": ffn, "mix": mix, "ple": ple, "attn": attention, "sgu": gating, "renorm": lambda n: None}[kind](n)

        @block.vector
        def _(dve):
            chain = [0]

            def link(ins):
                chain[0] += 1
                ins.then_inc(dve_chain, 1)
                dve.wait_ge(dve_chain, chain[0])

            def split(c, s=None):
                looped = s is not None
                if not looped and c >= TOTAL:
                    return
                if looped:
                    dve.wait_ge(hi_ready, c[0] + 1 + 3 * c[1])
                else:
                    s = c % SLOTS
                    dve.wait_ge(hi_ready, c + 1)
                dve.tensor_tensor(w_lo[:, s, :], raw[:, s, :], w_hi[:, s, :].bitcast(F32), ALU.subtract)\
                    .then_inc(lo_ready, 1)

            def low(out_lo, t, hi, shift=None):
                if shift is None:
                    return dve.tensor_tensor(out_lo, t, hi.bitcast(F32), ALU.subtract)
                return dve.scalar_tensor_tensor(out=out_lo, in0=t, scalar=shift, in1=hi.bitcast(F32),
                                                op0=ALU.add, op1=ALU.subtract)

            def norm(n):
                scale, shift = norm_cols(n)
                dve.wait_ge(rt_ready, n + 1)
                dve.reciprocal(rstd[:, 0:T], rt[:, 0:T]).then_inc(rstd_ready, 1)
                dve.wait_ge(rstd_ready, n + 1)
                if STAGES[n][0] == "renorm":
                    for k in range(KT):
                        dve.scalar_tensor_tensor(out=x[:, k, :], in0=x[:, k, :], scalar=scale(k), in1=rstd[:, 0:T],
                                                 op0=ALU.mult, op1=ALU.mult).then_inc(x_ready, 1)
                    return
                s = 8 * SPLIT_NO[n]

                def lower(k):
                    dve.wait_ge(xhi_ready, s + k + 1)
                    low(xs_lo[:, k, :], xn[:, k, :], xs_hi[:, k, :], shift and shift(k)).then_inc(xs_ready, 1)

                for k in range(KT):
                    dve.scalar_tensor_tensor(out=xn[:, k, :], in0=x[:, k, :], scalar=scale(k), in1=rstd[:, 0:T],
                                             op0=ALU.mult, op1=ALU.mult).then_inc(t_ready, 1)
                    if k:
                        lower(k - 1)
                lower(KT - 1)

            def ffn(n):
                f, c0 = FFN_NO[n], BASE[n]
                s0 = STEPS * f
                layer, first = f // 2, (f % 2) * LOOPED

                def gu_mul(s, c):
                    dve.wait_ge(chunks_done, c + 1)
                    dve.wait_ge(silu_done, s0 + s + 1)
                    if not (isinstance(s, int) and s0 + s == 0):
                        dve.wait_ge(gulo_ready, s0 + s)
                    dve.tensor_tensor(gu[:, :], bank[UP][:, :], silu_g[:, :], ALU.mult).then_inc(gu_ready, 1)

                def gu_low(s):
                    dve.wait_ge(guhi_ready, s0 + s + 1)
                    low(gu_lo[:, :], gu[:, :], gu_hi[:, :]).then_inc(gulo_ready, 1)

                def ada_half(i, half):
                    done = 8 * LOOPED * f + 8 * i
                    dve.wait_ge(ada_in[half], 16 * (i + LOOPED * f) + 16)
                    for m in range(4):
                        k = 4 * half + m
                        w = ada[:, half, m * ADA_W:(m + 1) * ADA_W]
                        if k == 0:
                            dve.tensor_scalar(ada_acc[:, :], w, c_act[:, 0:1], None, ALU.mult).then_inc(ada_step, 1)
                        else:
                            dve.wait_ge(ada_step, done + k)
                            dve.scalar_tensor_tensor(out=ada_acc[:, :], in0=w, scalar=c_act[:, k:k + 1],
                                                     in1=ada_acc[:, :], op0=ALU.mult, op1=ALU.add)\
                                .then_inc(ada_step, 1)

                def ada_store(i):
                    at = (i + first) * 4
                    dve.wait_ge(ada_summed, i + LOOPED * f + 1)
                    dve.tensor_tensor(mod[:, layer, bass.ds(at, 4)], bank[MISC][:, 0:4],
                                      cols[:, bass.ds(at + COLS["ada_b_2"][0] + 72 * layer, 4)], ALU.add)\
                        .then_inc(ada_stored, 1)

                split(c0 + 2)
                split(c0 + 3)
                gu_mul(0, c0 + 1)
                gu_low(0)
                split(c0 + 4)
                split(c0 + 5)
                gu_mul(1, c0 + 3)
                cl = c0 + 5
                with dve.Fori(0, LOOPED) as i:
                    split((cl + 1, i), (cl + 1) % SLOTS)
                    gu_low(i + 1)
                    split((cl + 2, i), (cl + 2) % SLOTS)
                    if f < 4:
                        ada_half(i, 0)
                    split((cl + 3, i), (cl + 3) % SLOTS)
                    if f < 4:
                        ada_half(i, 1)
                    gu_mul(i + 2, cl + 3 * i + 1)
                    if f < 4:
                        ada_store(i)
                split(c0 + 33)
                gu_low(STEPS - 1)
                split(c0 + 34)
                residual(n, lambda b: (bank_done, 3 * f + b + 1) if b < 3 else (chunks_done, c0 + 33))

            def residual(n, done):
                kind = STAGES[n][0]
                layer, j = (0, n - 5) if n < 8 else (1, n - 9)
                for k in range(KT):
                    if k % 2 == 0:
                        dve.wait_ge(*done(k // 2))
                    src = bank[k // 2][:, (k % 2) * T:(k % 2 + 1) * T]
                    if n < 5:
                        factor = 0.5 if kind == "ffn" else 1.0
                    elif kind == "ffn":
                        factor = half_g[:, layer, 8 * (j // 2) + k:8 * (j // 2) + k + 1]
                    else:
                        factor = modc(layer, 5, k)
                    dve.scalar_tensor_tensor(out=x[:, k, :], in0=src, scalar=factor, in1=x[:, k, :],
                                             op0=ALU.mult, op1=ALU.add).then_inc(x_ready, 1)

            def projected(n, c):
                residual(n, lambda b: (chunks_done, c + b + 1))

            def modulation(layer):
                dve.wait_ge(ada_stored, ADA_BLOCKS * (layer + 1))
                for j, g in enumerate(("ln_ffn1_2", "ln_mix_2", "ln_ffn2_2")):
                    at = COLS[g][0] + 8 * layer
                    link(dve.scalar_tensor_tensor(out=a_col[:, layer, 8 * j:8 * j + 8],
                                                  in0=modc(layer, 3 * j + 1, 0, 8), scalar=one_col[:, :],
                                                  in1=cols[:, at:at + 8], op0=ALU.add, op1=ALU.mult))
                for j in range(2):
                    link(dve.tensor_scalar(half_g[:, layer, 8 * j:8 * j + 8], modc(layer, 6 * j + 2, 0, 8),
                                           0.5, None, ALU.mult))

            conv_step = [0]

            def conv(count):
                for _ in range(count):
                    i = conv_step[0]
                    if i >= CT * CONV:
                        return
                    pair, j, k = i // (2 * CONV), (i % (2 * CONV)) // 2, i % 2
                    k += 2 * pair
                    src = glu[:, k, j:j + T]
                    w = col("conv_w", k * CONV + j)
                    if j == 0:
                        dve.wait_ge(ev("glu_done"), pair + 1)
                        ins = dve.tensor_scalar(conv_y[:, k, :], src, w, col("conv_b", k), ALU.mult, ALU.add)
                    else:
                        dve.wait_ge(ev("conv_step"), i - 1)
                        ins = dve.scalar_tensor_tensor(out=conv_y[:, k, :], in0=src, scalar=w, in1=conv_y[:, k, :],
                                                       op0=ALU.mult, op1=ALU.add)
                    ins.then_inc(ev("conv_step"), 1)
                    conv_step[0] += 1

            def mix(n):
                c = BASE[n]
                split(c + 2)
                split(c + 3)

                def gated(pair):
                    dve.wait_ge(ev("glu_pad"), 1)
                    dve.wait_ge(ev("conv_sig"), pair + 1)
                    dve.tensor_tensor(glu[:, 2 * pair:2 * pair + 2, CONV - 1:],
                                      bank[2 * pair][:, :].rearrange("p (a n) -> p a n", a=2),
                                      silu_g[:, :].rearrange("p (a n) -> p a n", a=2), ALU.mult)\
                        .then_inc(ev("glu_done"), 1)

                gated(0)
                split(c + 4)
                conv(8)
                split(c + 5)
                gated(1)
                split(c + 6)
                conv(8)
                split(c + 7)
                conv(8)
                split(c + 8)
                conv(6)
                dve.wait_ge(ev("la_act"), 3)
                dve.scalar_tensor_tensor(out=log_a, in0=bank[STAT][:, :], scalar=zero_col[:, :], in1=e_pos,
                                         op0=ALU.min, op1=ALU.subtract).then_inc(ev("log_a"), 1)
                split(c + 9)
                conv(6)
                dve.wait_ge(ev("e_done"), 2)
                dve.tensor_copy(cum_end, bank[MISC][:, :].rearrange("p (i t) -> p i t", t=CHUNK)[:, :, CHUNK - 1])\
                    .then_inc(ev("cum_end"), 1)
                dve.wait_ge(ev("qk_copied"), 2)
                for o, i0, i1 in ((q_dec, q_s, e_pos), (k_neg, k_s, e_neg), (q_neg, q_s, e_neg), (k_pos, k_s, e_pos)):
                    dve.tensor_tensor(o, i0, i1, ALU.mult).then_inc(ev("qk_scaled"), 1)
                split(c + 10)
                dve.wait_ge(ev("k_exp"), 8)
                dve.tensor_tensor(k_end, k_s, k_exp, ALU.mult).then_inc(ev("k_end"), 1)
                split(c + 11)
                conv(8)
                split(c + 12)
                for par in range(2):
                    dve.wait_ge(ev("scored"), par + 1)
                    dve.wait_ge(ev("score_zero"), 2)
                    for i, (m, b) in enumerate(((low_mask, 4 + par), (up_mask, 2 + par))):
                        if i:
                            dve.wait_ge(ev("score_sel"), 2 * par + 1)
                        dve.copy_predicated(score[par], m.bitcast(I32).unsqueeze(1).to_broadcast([P, 4, P]),
                                            bank[b][:, :].rearrange("p (n t) -> p n t", n=4)).then_inc(ev("score_sel"), 1)
                dve.wait_ge(ev("kv_done"), 1)
                dve.wait_ge(ev("decay"), 1)
                dve.tensor_copy(state[:, 0, :, :], bank[0][:, 0:T].rearrange("p (h v) -> p h v", h=2))\
                    .then_inc(ev("state"), 1)
                for i, src in ((1, bank[1][:, 0:T]), (2, bank[0][:, T:2 * T])):
                    for h in range(2):
                        dve.wait_ge(ev("state"), 2 * i - 1)
                        dve.scalar_tensor_tensor(out=state[:, i, h, :], in0=state[:, i - 1, h, :],
                                                 scalar=decay[:, 4 * h + i:4 * h + i + 1],
                                                 in1=src[:, h * P:(h + 1) * P], op0=ALU.mult, op1=ALU.add)\
                            .then_inc(ev("state"), 1)
                conv(16)
                for par in range(2):
                    dve.wait_ge(ev("o_rt"), par + 1)
                    root = silu_g if par else rt
                    link(dve.reciprocal(rstd[:, :], root[:, :]))
                    for hh in range(2):
                        h = 2 * hh + par
                        link(dve.scalar_tensor_tensor(out=xn[:, 4 + h, :], in0=bank[6 + par][:, hh * T:(hh + 1) * T],
                                                      scalar=col("gla_norm", h), in1=rstd[:, hh * T:(hh + 1) * T],
                                                      op0=ALU.mult, op1=ALU.mult))
                dve.wait_ge(ev("silu_r"), 2)
                for h in range(HG):
                    dve.tensor_tensor(xn[:, 4 + h, :], xn[:, 4 + h, :], silu_r[:, h, :], ALU.mult).then_inc(cs_t, 1)
                conv(CT * CONV)
                for h in range(HG):
                    dve.wait_ge(cs_hi_ready, h + 1)
                    low(cs_lo[:, 4 + h, :], xn[:, 4 + h, :], cs_hi[:, 4 + h, :]).then_inc(cs_ready, 1)
                dve.wait_ge(ev("ln_mean"), 1)
                dve.tensor_copy(rstd[:, 0:T], bank[0][:, 0:T]).then_inc(ev("ln_mean_copied"), 1)
                dve.wait_ge(ev("ln_mean_copied"), 1)
                dve.tensor_tensor(ub[:, 0:4, :], conv_y, rstd[:, 0:T].unsqueeze(1).to_broadcast([P, 4, T]), ALU.subtract)\
                    .then_inc(ev("ln_centred"), 1)
                dve.wait_ge(ev("ln_rt"), 1)
                link(dve.reciprocal(rstd[:, T:2 * T], rt[:, 0:T]))
                for k in range(CT):
                    dve.tensor_tensor(conv_y[:, k, :], ub[:, k, :], rstd[:, T:2 * T], ALU.mult).then_inc(ev("ln_t"), 1)
                for k in range(CT):
                    dve.wait_ge(cs_hi_ready, 4 + k + 1)
                    low(cs_lo[:, k, :], xn[:, k, :], cs_hi[:, k, :]).then_inc(cs_ready, 1)
                split(c + 13)
                split(c + 14)
                split(c + 15)
                projected(n, c + 10)

            def ple(n):
                c = BASE[n]
                dve.wait_ge(ev("p_hi"), 1)
                low(cs_lo[:, 0:2, :], ub[:, 0:2, :], cs_hi[:, 0:2, :]).then_inc(ev("p_lo"), 1)
                norm(n)
                split(c + 2)
                split(c + 3)
                for j in range(4):
                    dve.wait_ge(ev("ple_sig"), j + 1)
                    if j:
                        dve.wait_ge(x_ready, 8 * n + 2 * j)
                    dve.tensor_tensor(gu[:, :], bank[j][:, :], silu_g[:, :], ALU.mult).then_inc(ev("ple_mul"), 1)
                    dve.wait_ge(ev("ple_mul"), j + 1)
                    for k in (2 * j, 2 * j + 1):
                        dve.tensor_tensor(x[:, k, :], x[:, k, :], gu[:, (k % 2) * T:(k % 2 + 1) * T], ALU.add)\
                            .then_inc(x_ready, 1)
                    if j < 3:
                        split(c + 4 + j)

            def attention(n):
                c = BASE[n]

                def scored(i, j):
                    e = 2 * i + j
                    if not (isinstance(i, int) and i == 0 and j == 0):
                        dve.wait_ge(ev("attn"), 2 * e)
                    for comp in range(2):
                        dve.wait_ge(ev("logits"), e + 1)
                        dve.scalar_tensor_tensor(out=logit[:, comp, :], in0=bank[4 + comp][:, 0:SKEW], scalar=scale_col,
                                                 in1=bias_t[:, bass.ds(2 * i + j, 1), :].rearrange("p a j -> p (a j)"),
                                                 op0=ALU.mult, op1=ALU.add).then_inc(ev("logit"), 1)
                    dve.wait_ge(ev("logit"), 2 * e + 2)
                    for part in range(2):
                        dve.tensor_reduce(peak[:, 2 * part:2 * part + 2],
                                          logit[:, :, (P if part else 0):(SKEW if part else P)], AX_X, ALU.max,
                                          negate=True).then_inc(ev("peak2") if not part else ev("peak"), 1)

                def weights(i, j):
                    e = 2 * i + j
                    dve.wait_ge(ev("exp"), 4 * e + 4)
                    dve.reciprocal(recip, total).then_inc(ev("recip"), 1)
                    dve.wait_ge(ev("recip"), e + 1)
                    dve.tensor_tensor(coef, recip, lam_coef[:, :], ALU.mult).then_inc(ev("coef"), 1)
                    dve.wait_ge(ev("coef"), e + 1)
                    for part in range(2):
                        seg = slice(P, SKEW) if part else slice(0, P)
                        dve.tensor_scalar(logit[:, 1, seg], logit[:, 1, seg], coef[:, 2 * part + 1:2 * part + 2],
                                          None, ALU.mult).then_inc(ev("p1"), 1)
                    for part in range(2):
                        seg = slice(P, SKEW) if part else slice(0, P)
                        dve.wait_ge(ev("p1"), 2 * e + 1 + part)
                        if part == 0 and not (isinstance(i, int) and i == 0 and j == 0):
                            dve.wait_ge(ev("turned"), e)
                        dve.scalar_tensor_tensor(out=attn[:, seg], in0=logit[:, 0, seg],
                                                 scalar=coef[:, 2 * part:2 * part + 1], in1=logit[:, 1, seg],
                                                 op0=ALU.mult, op1=ALU.add).then_inc(ev("attn"), 1)

                def qk_out(i, which):
                    dve.wait_ge(ev("qk_rt"), 2 * i + which + 1)
                    if which or not isinstance(i, int):
                        dve.wait_ge(ev("qk_n"), 2 * i + which)
                    dve.reciprocal(rstd[:, :], rt[:, :]).then_inc(ev("qk_rstd"), 1)
                    dve.wait_ge(ev("qk_rstd"), 2 * i + which + 1)
                    dve.scalar_tensor_tensor(out=(q_n, k_n)[which], in0=(q_raw, k_raw)[which],
                                             scalar=col(("attn_q_norm_2", "attn_k_norm_2")[which]), in1=rstd[:, :],
                                             op0=ALU.mult, op1=ALU.mult).then_inc(ev("qk_n"), 1)

                def pair(i, before):
                    def sp_(m):
                        if isinstance(i, int):
                            split(c + 3 * i + m)
                        else:
                            split((c + 3 + m, i - 1), (c + 3 + m) % SLOTS)
                    sp_(2)
                    if before:
                        scored(i - 1, 0)
                    sp_(3)
                    if before:
                        weights(i - 1, 0)
                        scored(i - 1, 1)
                    qk_out(i, 0)
                    sp_(4)
                    if before:
                        weights(i - 1, 1)
                    qk_out(i, 1)

                dve.wait_ge(ev("bias_in"), 32)
                pair(0, False)
                with dve.Fori(1, 4) as i:
                    pair(i, True)
                split(c + 14)
                scored(3, 0)
                weights(3, 0)
                scored(3, 1)
                weights(3, 1)
                for j in range(4):
                    dve.wait_ge(ev("sub_rt"), j + 1)
                    if j:
                        dve.wait_ge(cs_t, 4 + 2 * j)
                    dve.reciprocal(rstd[:, :], rt[:, :]).then_inc(ev("sub_rstd"), 1)
                    dve.wait_ge(ev("sub_rstd"), j + 1)
                    dve.scalar_tensor_tensor(out=rstd[:, :], in0=bank[j][:, :], scalar=ms_limit[:, :], in1=rstd[:, :],
                                             op0=ALU.is_le, op1=ALU.mult).then_inc(ev("sub_kept"), 1)
                    dve.wait_ge(ev("sub_kept"), j + 1)
                    for k in (2 * j, 2 * j + 1):
                        dve.scalar_tensor_tensor(out=ub[:, k, :], in0=xn[:, k, :], scalar=sub_g[:, :],
                                                 in1=rstd[:, (k % 2) * T:(k % 2 + 1) * T], op0=ALU.mult, op1=ALU.mult)\
                            .then_inc(cs_t, 1)
                for k in range(KT):
                    dve.wait_ge(cs_hi_ready, 8 + k + 1)
                    low(cs_lo[:, k, :], ub[:, k, :], cs_hi[:, k, :]).then_inc(cs_ready, 1)
                split(c + 15)
                split(c + 16)
                split(c + 17)
                projected(n, c + 12)

            def gating(n):
                c = BASE[n]
                dve.wait_ge(ev("sgu_in"), 64)
                dve.tensor_tensor(w_mix, w_mix, causal.unsqueeze(1).to_broadcast([P, KT, P]), ALU.mult)\
                    .then_inc(ev("w_mix"), 1)
                for j in range(5):
                    split(c + 2 + j)
                dve.wait_ge(ev("v_gelu"), 4)
                link(dve.tensor_reduce(v_sum, v_g, AX_X, ALU.add))
                link(dve.tensor_scalar(v_mean, v_sum, 1.0 / D, None, ALU.mult))
                for t in range(2):
                    dve.tensor_scalar(v_g[:, t, :], v_g[:, t, :], v_mean[:, t:t + 1], None, ALU.subtract)\
                        .then_inc(ev("v_centred"), 1)
                split(c + 7)
                split(c + 8)
                dve.wait_ge(ev("v_rt"), 1)
                link(dve.reciprocal(v_rstd, v_rt))
                for t in range(2):
                    dve.scalar_tensor_tensor(out=v_g[:, t, :], in0=v_g[:, t, :], scalar=v_rstd[:, t:t + 1],
                                             in1=ln_rows[:, 0, :], op0=ALU.mult, op1=ALU.mult).then_inc(ev("v_scaled"), 1)
                for t in range(2):
                    dve.wait_ge(ev("v_scaled"), t + 1)
                    dve.tensor_tensor(v_g[:, t, :], v_g[:, t, :], ln_rows[:, 1, :], ALU.add).then_inc(ev("v_norm"), 1)
                split(c + 9)
                split(c + 10)
                for j in range(4):
                    dve.wait_ge(ev("mixed"), j + 1)
                    for k in (2 * j, 2 * j + 1):
                        dve.tensor_tensor(xn[:, k, :], bank[j][:, (k % 2) * T:(k % 2 + 1) * T], ub[:, k, :], ALU.mult)\
                            .then_inc(cs_t, 1)
                for k in range(KT):
                    dve.wait_ge(cs_hi_ready, 16 + k + 1)
                    low(cs_lo[:, k, :], xn[:, k, :], cs_hi[:, k, :]).then_inc(cs_ready, 1)
                split(c + 11)
                split(c + 12)
                split(c + 13)
                projected(n, c + 8)

            scale_col = 0.125
            dve.wait_ge(ev("lam_in"), 16)
            dve.tensor_tensor(lam_in[:, 4:6], lam_in[:, 0:4:2], lam_in[:, 1:4:2], ALU.mult).then_inc(ev("lam_prod"), 1)
            dve.wait_ge(memsets, 8)
            dve.wait_ge(ev("table_in"), 32)
            for h in range(HA):
                if h:
                    dve.wait_ge(ev("skew_mm"), h)
                dve.tensor_scalar(table_b, ones_1[0:NB + 1, :], table[:, h:h + 1], None, ALU.mult)\
                    .then_inc(ev("table_b"), 1)
                dve.wait_ge(ev("skew_mm"), h + 1)
                dve.tensor_copy(bias_t[:, h, :], bank[h % 4][:, 0:SKEW]).then_inc(ev("skew_copied"), 1)
            dve.wait_ge(ev("lam_exp"), 1)
            link(dve.tensor_tensor(nlam[:, :], lam_e[:, 1:2], lam_e[:, 0:1], ALU.subtract))
            link(dve.tensor_scalar(nlam[:, :], nlam[:, :], -LAMBDA_INIT, None, ALU.add))
            link(dve.scalar_tensor_tensor(out=lam_size[:, :], in0=nlam[:, :], scalar=-1.0, in1=nlam[:, :],
                                          op0=ALU.mult, op1=ALU.max))
            link(dve.tensor_scalar(lam_size[:, :], lam_size[:, :], 1.0, None, ALU.max))
            link(dve.reciprocal(lam_r[:, :], lam_size[:, :]))
            for i in range(2):
                link(dve.tensor_copy(lam_coef[:, 2 * i:2 * i + 1], lam_r[:, :]))
                link(dve.tensor_tensor(lam_coef[:, 2 * i + 1:2 * i + 2], lam_r[:, :], nlam[:, :], ALU.mult))
            link(dve.tensor_tensor(eps_sub[:, :], lam_r[:, :], lam_r[:, :], ALU.mult))
            link(dve.tensor_scalar(eps_sub[:, :], eps_sub[:, :], EPS, TINY, ALU.mult, ALU.max))
            link(dve.tensor_scalar(ms_limit[:, :], lam_r[:, :], FLT_MAX / P, lam_r[:, :], ALU.mult, ALU.mult))
            dve.wait_ge(consts_in, 32)
            link(dve.tensor_scalar(sub_g[:, :], col("attn_subln_2"), 1.0 - LAMBDA_INIT, None, ALU.mult))
            dve.wait_ge(ev("c_act"), 1)
            split(0)
            split(1)
            norm(0)
            for n, (kind, _) in enumerate(STAGES):
                if n in (5, 9):
                    modulation(n // 9)
                if n and kind != "ple":
                    norm(n)
                {"ffn": ffn, "mix": mix, "ple": ple, "attn": attention, "sgu": gating, "renorm": lambda n: None}[kind](n)

        @block.tensor
        def _(pe):
            def mm3(out_, a_hi, a_lo, b_hi, b_lo, start, stop):
                pe.matmul(out_, a_hi, b_hi, start=start, stop=False, skip_group_check=True)
                pe.matmul(out_, a_hi, b_lo, start=False, stop=False, skip_group_check=True)
                return pe.matmul(out_, a_lo, b_hi, start=False, stop=stop, skip_group_check=True)

            def arrived(c):
                pe.wait_ge(hi_ready, c + 1)
                pe.wait_ge(lo_ready, c + 1)

            def wide(s, b, hi, lo, each=None):
                wh, wl = lin(s, w_hi), lin(s, w_lo)
                for nb in range(2):
                    for k in range(KT):
                        if each is not None and nb == 0:
                            pe.wait_ge(each[0], each[1] + k + 1)
                        ins = mm3(bank[b][:, nb * T:(nb + 1) * T], wh[:, k, nb * P:(nb + 1) * P],
                                  wl[:, k, nb * P:(nb + 1) * P], hi[:, k, :], lo[:, k, :], k == 0, k == KT - 1)
                ins.then_inc(chunks_done, 1)

            def token_major(s, b):
                wh, wl = lin(s, w_hi), lin(s, w_lo)
                for t in range(2):
                    for k in range(KT):
                        ins = mm3(bank[b][:, t * NC:(t + 1) * NC], xs_hi[:, k, t * P:(t + 1) * P],
                                  xs_lo[:, k, t * P:(t + 1) * P], wh[:, k, :], wl[:, k, :], k == 0, k == KT - 1)
                ins.then_inc(chunks_done, 1)

            def over_two(s, hi, lo, first, last, f=None, between=None):
                wh, wl = tail(s, w_hi), tail(s, w_lo)
                for nb in range(KT):
                    o = bank[nb // 2][:, (nb % 2) * T:(nb % 2 + 1) * T]
                    for j in range(2):
                        ins = mm3(o, wh[:, j, nb * P:(nb + 1) * P], wl[:, j, nb * P:(nb + 1) * P],
                                  hi(j), lo(j), first and j == 0 and nb % 2 == 0, last and j == 1)
                    if last and f is not None and nb % 2 and nb < KT - 1:
                        ins.then_inc(bank_done, 1)
                    if nb == 1 and between is not None:
                        between()
                ins.then_inc(chunks_done, 1)

            def norm(n):
                for k in range(KT):
                    pe.wait_ge(sq_ready, 8 * n + k + 1)
                    ins = pe.matmul(bank[STAT][:, 0:T], ones_d[:, :], xn[:, k, :], start=(k == 0), stop=(k == KT - 1),
                                    skip_group_check=True)
                ins.then_inc(ss_ready, 1)

            def ffn(n):
                f, c0 = FFN_NO[n], BASE[n]
                s0 = STEPS * f
                xw = (xs_ready, 8 * SPLIT_NO[n])
                g_half = (lambda j: gu_hi[:, j * T:(j + 1) * T]), (lambda j: gu_lo[:, j * T:(j + 1) * T])

                arrived(c0)
                wide(c0 % SLOTS, GATE, xs_hi, xs_lo, xw)
                arrived(c0 + 1)
                wide((c0 + 1) % SLOTS, UP, xs_hi, xs_lo)
                arrived(c0 + 2)
                pe.wait_ge(silu_done, s0 + 1)
                wide((c0 + 2) % SLOTS, GATE, xs_hi, xs_lo)
                arrived(c0 + 3)
                pe.wait_ge(gu_ready, s0 + 1)
                wide((c0 + 3) % SLOTS, UP, xs_hi, xs_lo)
                arrived(c0 + 4)
                pe.wait_ge(gulo_ready, s0 + 1)
                over_two((c0 + 4) % SLOTS, *g_half, True, False)
                cl = c0 + 5
                with pe.Fori(0, LOOPED) as i:
                    arrived(cl + 3 * i)
                    pe.wait_ge(silu_done, s0 + 2 + i)
                    wide(cl % SLOTS, GATE, xs_hi, xs_lo)
                    arrived(cl + 1 + 3 * i)
                    pe.wait_ge(gu_ready, s0 + 2 + i)
                    wide((cl + 1) % SLOTS, UP, xs_hi, xs_lo)
                    arrived(cl + 2 + 3 * i)
                    pe.wait_ge(gulo_ready, s0 + 2 + i)

                    def ada_sum():
                        pe.wait_ge(ada_step, 8 * LOOPED * f + 8 + 8 * i)
                        for j in range(4):
                            ins = pe.matmul(bank[MISC][:, j:j + 1], ada_acc[:, j * P:(j + 1) * P], ones_1[:, 0:1],
                                            start=True, stop=True, skip_group_check=True)
                        ins.then_inc(ada_summed, 1)

                    over_two((cl + 2) % SLOTS, *g_half, False, False, between=ada_sum if f < 4 else None)
                arrived(c0 + 32)
                pe.wait_ge(gulo_ready, s0 + STEPS)
                over_two((c0 + 32) % SLOTS, *g_half, False, True, f)

            def outputs(c, cs):
                for j in range(4):
                    arrived(c + j)
                    wide((c + j) % SLOTS, j, cs_hi, cs_lo, (cs_ready, cs) if j == 0 else None)

            def mix(n):
                c = BASE[n]
                for j in range(10):
                    arrived(c + j)
                    if j in (6, 7):
                        pe.wait_ge(ev("glu_done"), 1)
                        token_major((c + j) % SLOTS, j - 6)
                    else:
                        if j in (8, 9):
                            pe.wait_ge(ev("glu_done"), 2)
                        wide((c + j) % SLOTS, (0, 1, 2, 3, 4, 5, None, None, 2, 3)[j], xs_hi, xs_lo,
                             (xs_ready, 8 * SPLIT_NO[n]) if j == 0 else None)
                    if j == 5:
                        pe.wait_ge(ev("gate_w_in"), 48)
                        for k in range(KT):
                            ins = pe.matmul(bank[MISC][0:16, 0:T], w_glr[:, k, :], xn[:, k, :], start=(k == 0),
                                            stop=(k == KT - 1), skip_group_check=True)
                        ins.then_inc(ev("glr_done"), 1)
                    if j == 6:
                        pe.wait_ge(ev("glr_copied"), 1)
                        for t in range(2):
                            ins = pe.matmul(bank[STAT][:, t * T:(t + 1) * T], glr[0:17, t * P:(t + 1) * P], wup[0:17, :],
                                            start=(t == 0), stop=True, skip_group_check=True)
                        ins.then_inc(ev("z_done"), 1)
                    if j == 7:
                        pe.wait_ge(ev("log_a"), 1)
                        for h in range(2):
                            for t in range(2):
                                ins = pe.matmul(bank[MISC][:, h * T + t * P:h * T + (t + 1) * P],
                                                log_a[:, t * T + h * P:t * T + (h + 1) * P], tri,
                                                start=(h == 0 and t == 0), stop=True, skip_group_check=True)
                        ins.then_inc(ev("cum_done"), 1)
                pe.wait_ge(ev("k_end"), 1)
                pe.wait_ge(ev("log_a"), 1)
                for t in range(2):
                    for h in range(2):
                        ins = pe.matmul(bank[STAT][:, t * T + h * P:t * T + (h + 1) * P],
                                        k_end[:, h * T + t * P:h * T + (t + 1) * P], ident, is_transpose=True,
                                        start=(t == 0 and h == 0), stop=True, skip_group_check=True)
                ins.then_inc(ev("ke_turned"), 1)
                pe.wait_ge(ev("qk_scaled"), 4)
                pe.wait_ge(ev("silu_r"), 2)
                for par in range(2):
                    r = slice(64 * par, 64 * par + 64)
                    for b, k_, q_ in ((4 + par, k_neg, q_dec), (2 + par, k_pos, q_neg)):
                        for hh in range(2):
                            for t in range(2):
                                at = hh * T + t * P
                                ins = pe.matmul(bank[b][:, at:at + P], k_[r, at:at + P], q_[r, at:at + P],
                                                start=(hh == 0 and t == 0), stop=True, skip_group_check=True)
                    ins.then_inc(ev("scored"), 1)
                pe.wait_ge(ev("ke_copied"), 1)
                pe.wait_ge(ev("v_copied"), 2)
                for i in range(3):
                    r = slice(CHUNK * (i % 2), CHUNK * (i % 2) + CHUNK)
                    for h in range(HG):
                        o = bank[i % 2][64 * (h % 2):64 * (h % 2) + 64, (i // 2) * T + (h // 2) * P:(i // 2) * T + (h // 2 + 1) * P]
                        ins = pe.matmul(o, ke_t[r, i // 2, h * 64:(h + 1) * 64],
                                        v_tok[r, h // 2, i // 2, (h % 2) * P:(h % 2 + 1) * P],
                                        start=(i < 2 and h < 2), stop=True, skip_group_check=True)
                ins.then_inc(ev("kv_done"), 1)
                for par in range(2):
                    r = slice(64 * par, 64 * par + 64)
                    pe.wait_ge(ev("score_sel"), 2 * par + 2)
                    for hh in range(2):
                        for t in range(2):
                            pe.matmul(bank[6 + par][:, hh * T + t * P:hh * T + (t + 1) * P],
                                      v_tok[:, hh, t, par * P:(par + 1) * P], score[par][:, 2 * hh + t, :],
                                      start=(hh == 0 and t == 0), stop=False, skip_group_check=True)
                    pe.wait_ge(ev("state"), 5)
                    for hh in range(2):
                        for i in range(1, 4):
                            at = hh * T + i * CHUNK
                            ins = pe.matmul(bank[6 + par][:, at:at + CHUNK], state[r, i - 1, hh, :],
                                            q_dec[r, at:at + CHUNK], start=False, stop=True, skip_group_check=True)
                    ins.then_inc(ev("o_done"), 1)
                for par in range(2):
                    pe.wait_ge(ev("o_sq"), par + 1)
                    pe.matmul(bank[4 + par][:, :], ones_v[:, :], ub[:, 4 + 2 * par:6 + 2 * par, :], start=True, stop=True,
                              skip_group_check=True).then_inc(ev("o_ms"), 1)
                pe.wait_ge(ev("conv_step"), CT * CONV)
                for k in range(CT):
                    ins = pe.matmul(bank[0][:, 0:T], ones_c[:, :], conv_y[:, k, :], start=(k == 0), stop=(k == CT - 1),
                                    skip_group_check=True)
                ins.then_inc(ev("ln_mean"), 1)
                pe.wait_ge(ev("ln_sq"), 1)
                for k in range(CT):
                    ins = pe.matmul(bank[1][:, 0:T], ones_c[:, :], conv_y[:, k, :], start=(k == 0), stop=(k == CT - 1),
                                    skip_group_check=True)
                ins.then_inc(ev("ln_var"), 1)
                pe.wait_ge(cs_ready, 8)
                outputs(c + 10, 0)

            def ple(n):
                c = BASE[n]
                pe.wait_ge(ev("p_lo"), 1)
                arrived(c)
                over_two(c % SLOTS, lambda j: cs_hi[:, j, :], lambda j: cs_lo[:, j, :], True, True)
                norm(n)
                for j in range(4):
                    arrived(c + 1 + j)
                    if j >= 2:
                        pe.wait_ge(ev("ple_sig"), j - 1)
                    wide((c + 1 + j) % SLOTS, 4 + j % 2, xs_hi, xs_lo, (xs_ready, 8 * SPLIT_NO[n]) if j == 0 else None)

            def attention(n):
                c = BASE[n]

                def logits(i, j):
                    e = 2 * i + j
                    pe.wait_ge(ev("qk_n"), 2 * i + 2)
                    if not (isinstance(i, int) and i == 0 and j == 0):
                        pe.wait_ge(ev("logit"), 2 * e)
                    for comp in range(2):
                        r = slice(64 * comp, 64 * comp + 64)
                        pe.matmul(bank[4 + comp][:, 0:P], q_n[r, j * T:j * T + P], k_n[r, j * T:j * T + P],
                                  start=True, stop=True, skip_group_check=True)
                        ins = pe.matmul(bank[4 + comp][:, P:SKEW], q_n[r, j * T + P:(j + 1) * T], k_n[r, j * T:(j + 1) * T],
                                        start=False, stop=True, skip_group_check=True)
                    ins.then_inc(ev("logits"), 1)

                def turn(i, j):
                    e = 2 * i + j
                    pe.wait_ge(ev("attn"), 2 * e + 2)
                    for m in range(3):
                        ins = pe.matmul(bank[MISC][:, m * P:(m + 1) * P], attn[:, m * P:(m + 1) * P], ident,
                                        is_transpose=True, start=(m == 0), stop=True, skip_group_check=True)
                    ins.then_inc(ev("turned"), 1)

                def out(i, j):
                    e = 2 * i + j
                    pe.wait_ge(ev("turned_copied"), e + 1)
                    pe.wait_ge(ev("va"), i + 1)
                    if j == 0 and not (isinstance(i, int) and i == 0):
                        pe.wait_ge(ev("o_copied"), i)
                    v = lambda t: va[:, t, j * P:(j + 1) * P]
                    o = bank[7]
                    pe.matmul(o[:, j * T:j * T + P], v(0), attn_t[:, 0:P], start=(j == 0), stop=True, skip_group_check=True)
                    pe.matmul(o[:, j * T + P:(j + 1) * T], v(0), attn_t[:, P:2 * P], start=False, stop=False,
                              skip_group_check=True)
                    ins = pe.matmul(o[:, j * T + P:(j + 1) * T], v(1), attn_t[:, 2 * P:3 * P], start=False, stop=True,
                                    skip_group_check=True)
                    if j == 1:
                        ins.then_inc(ev("pair_done"), 1)

                def square_sums(i, which):
                    pe.wait_ge(ev("qk_sq"), 2 * i + which + 1)
                    if which:
                        pe.wait_ge(ev("qk_rt"), 2 * i + 1)
                    pe.matmul(bank[3][:, :], pair_ones, qk_sq, start=True, stop=True, skip_group_check=True)\
                        .then_inc(ev("qk_norm_ms"), 1)

                def chunk(i, part, first=False):
                    cc = c + 3 * i + part
                    arrived(cc)
                    s = (c + part) % SLOTS
                    if part < 2:
                        if not first:
                            pe.wait_ge(ev("qk_raw"), 2 * i + part - 1)
                            pe.wait_ge(ev("qk_sq"), 2 * i + part - 1)
                        wide(s, part, xs_hi, xs_lo, (xs_ready, 8 * SPLIT_NO[n]) if first and part == 0 else None)
                    else:
                        if not first:
                            pe.wait_ge(ev("va"), i)
                        token_major(s, 2)

                def pair(i, before):
                    chunk(i, 0, not before)
                    if before:
                        logits(i - 1, 0)
                    chunk(i, 1, not before)
                    if before:
                        turn(i - 1, 0)
                        logits(i - 1, 1)
                        out(i - 1, 0)
                    square_sums(i, 0)
                    chunk(i, 2, not before)
                    if before:
                        turn(i - 1, 1)
                        out(i - 1, 1)
                    square_sums(i, 1)

                pair(0, False)
                with pe.Fori(1, 4) as i:
                    pair(i, True)
                logits(3, 0)
                turn(3, 0)
                logits(3, 1)
                out(3, 0)
                turn(3, 1)
                out(3, 1)
                for j in range(4):
                    pe.wait_ge(ev("sub_sq"), j + 1)
                    pe.matmul(bank[j][:, :], ones_v[:, :], ub[:, 2 * j:2 * j + 2, :], start=True, stop=True,
                              skip_group_check=True).then_inc(ev("sub_ms"), 1)
                pe.wait_ge(ev("sub_rt"), 4)
                outputs(c + 12, 8)

            def gating(n):
                c = BASE[n]
                for j in range(4):
                    arrived(c + j)
                    if j == 0:
                        pe.wait_ge(xs_ready, 8 * SPLIT_NO[n] + 8)
                    token_major((c + j) % SLOTS, j)
                for j in range(4):
                    arrived(c + 4 + j)
                    if j >= 2:
                        pe.wait_ge(ev("u_gelu"), j - 1)
                    wide((c + 4 + j) % SLOTS, 4 + j % 2, xs_hi, xs_lo)
                pe.wait_ge(ev("w_mix"), 1)
                pe.wait_ge(ev("v_norm"), 2)
                for g in range(KT):
                    for t in range(2):
                        o = bank[g // 2][:, (g % 2) * T + t * P:(g % 2) * T + (t + 1) * P]
                        pe.matmul(o, v_g[:, t, g * P:(g + 1) * P], w_mix[:, g, :], start=(g % 2 == 0 and t == 0), stop=False,
                                  skip_group_check=True)
                        ins = pe.matmul(o, ones_1[0:1, :], b_mix[:, g, :], start=False, stop=True, skip_group_check=True)
                    if g % 2:
                        ins.then_inc(ev("mixed"), 1)
                pe.wait_ge(cs_t, 20)
                outputs(c + 8, 16)

            pe.wait_ge(memsets, 8)
            pe.wait_ge(ev("lam_prod"), 1)
            pe.matmul(bank[STAT][:, 0:2], ones_1[0:64, :], lam_in[:, 4:6], start=True, stop=True,
                      skip_group_check=True).then_inc(ev("lam_sum"), 1)
            for h in range(HA):
                pe.wait_ge(ev("table_b"), h + 1)
                if h >= 4:
                    pe.wait_ge(ev("skew_copied"), h - 3)
                pe.matmul(bank[h % 4][:, 0:SKEW], table_b, one_hot, start=True, stop=True,
                          skip_group_check=True).then_inc(ev("skew_mm"), 1)
            pe.wait_ge(ev("lam_exp"), 1)
            pe.wait_ge(consts_in, 32)
            pe.wait_ge(ev("skew_copied"), HA)
            for n, (kind, _) in enumerate(STAGES):
                if kind != "ple":
                    norm(n)
                {"ffn": ffn, "mix": mix, "ple": ple, "attn": attention, "sgu": gating, "renorm": lambda n: None}[kind](n)


HEAD_SCALE = CHUNK ** -0.5


def shape_constants():
    s, t = np.arange(P)[:, None], np.arange(P)[None, :]
    same = s // CHUNK == t // CHUNK
    consts = np.stack([
        np.where(same & (s <= t), 1 / 16, 0), same & (s <= t), same & (s > t), s == t, s <= t,
        np.where(s // 64 == t // 64, 1 / 64, 0),
    ], 1).astype(np.float32)
    one_hot = np.zeros((NB + 1, SKEW), np.float32)
    for m in range(SKEW):
        rel = T - 1 - m
        if rel < 0:
            b = NB
        elif rel < 16:
            b = rel
        else:
            b = min(NB - 1, 16 + int(np.floor(np.log2(rel / 16) / 3 * 16 + 1e-9)))
        one_hot[b, m] = 1
    return consts, one_hot


def kernel(**inputs):
    import concourse.bacc as bacc
    from concourse.bass_utils import run_bass_kernel_spmd

    a = {k: np.asarray(v) for k, v in inputs.items()}

    def tiles(v):
        v = v.reshape(-1, P)
        return v.T

    parts = {k: a[k] for k in COLS}
    parts["conv_w"] = a["conv_w"][0].T.reshape(CT, P, CONV).transpose(0, 2, 1)
    for k in ("attn_q_norm_2", "attn_k_norm_2"):
        parts[k] = np.concatenate([a[k][0], a[k][0]])
    consts, one_hot = shape_constants()
    arrays = {
        "x": a["x"][0].reshape(T, KT, P).transpose(2, 1, 0),
        "p": a["p"][0, 0].reshape(T, 2, P).transpose(2, 1, 0),
        "cols": np.concatenate([tiles(parts[k]) for k in COLS], 1),
        "lam": np.stack([a[k][0] for k in ("attn_lq1_2", "attn_lk1_2", "attn_lq2_2", "attn_lk2_2")], 1),
        "w_mix": a["sgu_w_s_2"][0].transpose(2, 0, 1),
        "consts": consts,
        "one_hot": one_hot,
    }
    for k in ("ffn1_w_in", "ffn1_w_out", "ffn2_w_in", "ffn2_w_out", "w_in", "w_out", "gate_w_up", "gate_b",
              "ple_w_gate", "ple_w_proj", "rel_bias_2", "ada_w_2", "ffn1_wg_2", "ffn1_wu_2", "ffn1_wd_2",
              "ffn2_wg_2", "ffn2_wu_2", "ffn2_wd_2", "attn_w_qkv_2", "attn_w_o_2", "sgu_w_in_2", "sgu_w_out_2",
              "sgu_ln_g_2", "sgu_ln_b_2", "sgu_b_s_2"):
        arrays[k] = a[k]
    arrays = {f"in_{k}": np.ascontiguousarray(v) for k, v in arrays.items()}
    nc = bacc.Bacc("TRN2", target_bir_lowering=False, num_devices=1)
    dram = {k[3:]: nc.dram_tensor(k, v.shape, mybir.dt.from_np(v.dtype), kind="ExternalInput").ap()
            for k, v in arrays.items()}
    out = nc.dram_tensor("out", (P, KT, T), F32, kind="ExternalOutput").ap()
    two_blocks(nc, dram, out)
    got = run_bass_kernel_spmd(nc, [arrays], core_ids=[0]).results[0]["out"]
    return got.reshape(P, KT, T).transpose(2, 1, 0).reshape(1, T, D)
```

```python
from contextlib import ExitStack

import numpy as np

import concourse.bass as bass
from concourse import mybir

ALU = mybir.AluOpType
ACT = mybir.ActivationFunctionType
F32 = mybir.dt.float32
F32R = mybir.dt.float32r
I32 = mybir.dt.int32
AX_X = mybir.AxisListType.X

P = 128
T = 256
D = 1024
KT = D // P
F = 2816
NC = 256
STEPS = F // NC
SLOTS = 3
CH = KT * NC
EPS = 1e-6
CONV = 31
CT = 4
HG = 4
CHUNK = 64
HA = 8
HEAD_SCALE = CHUNK ** -0.5
FILL = 2
LN_EXP = "natural_log_exp_and_others"
NB = 32
LAMBDA_INIT = 0.2
FLT_MAX = float(np.finfo(np.float32).max)
TINY = 1e-36
ADA_W = 512
ADA_BLOCKS = 9 * D // ADA_W
LOOPED = STEPS - 2
assert ADA_BLOCKS == 2 * LOOPED and CH == 2 * D

STAGES = [("ffn", 33), ("mix", 14), ("ffn", 33), ("ple", 5), ("renorm", 0),
          ("ffn", 33), ("attn", 16), ("ffn", 33), ("renorm", 0),
          ("ffn", 33), ("sgu", 12), ("ffn", 33), ("renorm", 0)]
BASE = [sum(c for _, c in STAGES[:n]) for n in range(len(STAGES))]
TOTAL = sum(c for _, c in STAGES)
POOLED = [0 if n == 0 else c - (k == "mix") if k in ("mix", "attn", "sgu") else min(c, 2)
          for n, (k, c) in enumerate(STAGES)]
SPLIT_NO = [sum(k != "renorm" for k, _ in STAGES[:n]) for n in range(len(STAGES))]
PAIRED = [n > 0 and STAGES[n - 1][0] not in ("renorm", "ple") for n in range(len(STAGES))]
PAIRED_NO = [sum(PAIRED[:n]) for n in range(len(STAGES))]
FFN_NO = [sum(k == "ffn" for k, _ in STAGES[:n]) for n in range(len(STAGES))]

COLS = {}
_at = 0
for _name, _n in [("ffn1_norm", 8), ("mix_norm", 8), ("ffn2_norm", 8), ("ple_norm", 8), ("final_norm", 8),
                  ("ln_ffn1_2", 16), ("ln_mix_2", 16), ("ln_ffn2_2", 16), ("ln_out_2", 16),
                  ("conv_b", 4), ("conv_ln_g", 4), ("conv_ln_b", 4), ("gla_norm", 4), ("conv_w", 4 * CONV),
                  ("attn_q_norm_2", 1), ("attn_k_norm_2", 1), ("attn_subln_2", 1), ("c_2", 8),
                  ("ada_b_2", 144)]:
    COLS[_name] = (_at, _n)
    _at += _n
NCOLS = _at
X_PARTS = 4
SKEW = 384


def two_blocks(nc, a, out):
    with ExitStack() as ctx:
        def sb(name, shape, dt=F32):
            return ctx.enter_context(nc.sbuf_tensor(name, shape, dt))

        def sem(name):
            return ctx.enter_context(nc.semaphore(name))

        raw = sb("raw", [P, SLOTS, CH])
        w_hi = sb("w_hi", [P, SLOTS, CH], F32R)
        w_lo = sb("w_lo", [P, SLOTS, CH], F32R)
        x = sb("x_res", [P, KT, T])
        xs_hi = sb("xs_hi", [P, KT, T], F32R)
        xs_lo = sb("xs_lo", [P, KT, T], F32R)
        cs_hi = sb("cs_hi", [P, KT, T], F32R)
        cs_lo = sb("cs_lo", [P, KT, T], F32R)
        last_hi = cs_hi[:, 6:8, :].rearrange("p a n -> p (a n)")
        last_lo = cs_lo[:, 6:8, :].rearrange("p a n -> p (a n)")
        xn = sb("xn", [P, KT, T])
        ub = sb("ub", [P, KT, T])
        ada = sb("ada", [P, 2, 4 * ADA_W])
        ada_acc = sb("ada_acc", [P, ADA_W])
        silu_g = sb("silu_g", [P, 2 * T])
        gu = sb("gu", [P, 2 * T])
        gu_hi = sb("gu_hi", [P, 2 * T], F32R)
        gu_lo = sb("gu_lo", [P, 2 * T], F32R)
        rstd = sb("rstd", [P, 2 * T])
        cols = sb("cols_sb", [P, NCOLS])
        consts = sb("consts_sb", [P, 6, P])
        tri, low_mask, up_mask, ident, causal, pair_ones = (consts[:, i, :] for i in range(6))
        ones_d = sb("ones_d", [P, P])
        ones_c = sb("ones_c", [P, P])
        ones_v = sb("ones_v", [P, P])
        ones_1 = sb("ones_1", [P, P])
        eps_col = sb("eps_col", [P, 1])
        one_col = sb("one_col", [P, 1])
        zero_col = sb("zero_col", [P, 1])
        c_act = sb("c_act", [P, KT])
        mod = sb("mod", [P, 2, 72])
        a_col = sb("a_col", [P, 2, 3 * KT])
        half_g = sb("half_g", [P, 2, 2 * KT])
        nlam = sb("nlam", [P, 1])
        lam_size = sb("lam_size", [P, 1])
        lam_r = sb("lam_r", [P, 1])
        lam_coef = sb("lam_coef", [P, 4])
        eps_sub = sb("eps_sub", [P, 1])
        ms_limit = sb("ms_limit", [P, 1])
        lam_in = sb("lam_in", [64, 8])
        lam_e = sb("lam_e", [P, 2])
        sub_g = sb("sub_g", [P, 1])
        ARENA = 9912
        arena = sb("arena", [P, ARENA])
        top = [0]

        def carve(n, rows=P):
            top[0] += n
            assert top[0] <= ARENA, top[0]
            return arena[0:rows, top[0] - n:top[0]]

        glu = carve(CT * (T + CONV - 1)).rearrange("p (c t) -> p c t", c=CT)
        conv_y = carve(CT * T).rearrange("p (c t) -> p c t", c=CT)
        q_s, k_s, log_a, e_pos, e_neg, k_exp = (carve(2 * T) for _ in range(6))
        ke_t = carve(2 * T).rearrange("p (a n) -> p a n", a=2)
        score = [carve(2 * T).rearrange("p (n t) -> p n t", n=4) for _ in range(2)]
        state = carve(3 * 2 * P).rearrange("p (c h v) -> p c h v", c=3, h=2)
        v_tok = carve(4 * T).rearrange("p (m a n) -> p m a n", m=2, a=2)
        o_rstd = [q_s, e_pos]
        ln_mean_s, ln_rstd_s = carve(T), carve(T)
        glr = carve(T, 32)
        wup = carve(T, 32)
        w_glr = carve(KT * 16).rearrange("p (k n) -> p k n", k=KT)
        cum_end = carve(8)
        decay = carve(8)
        ada_flat = ada[:, :, :].rearrange("p a n -> p (a n)")
        q_dec, k_neg, q_neg, k_pos, k_end = (ada_flat[:, i * 2 * T:(i + 1) * 2 * T] for i in range(5))
        silu_r = ada_flat[:, 10 * T:14 * T].rearrange("p (c t) -> p c t", c=4)
        top[0] = 0
        bias_t = carve(HA * SKEW).rearrange("p (h j) -> p h j", h=HA)
        q_raw, k_raw, qk_sq, q_n, k_n = (carve(2 * T) for _ in range(5))
        va = carve(2 * T).rearrange("p (a n) -> p a n", a=2)
        logit = carve(2 * SKEW).rearrange("p (c j) -> p c j", c=2)
        attn = carve(SKEW)
        attn_t = carve(SKEW)
        peak, total, recip, coef = (carve(4) for _ in range(4))
        sub_rstd = [carve(2 * T) for _ in range(4)]
        top[0] = 0
        table = carve(HA, NB + 1)
        one_hot = carve(SKEW, NB + 1)
        rows = carve(SKEW, HA)
        top[0] = 0
        ln_rows = carve(2 * D).rearrange("p (a n) -> p a n", a=2)
        w_mix = carve(KT * P).rearrange("p (g t) -> p g t", g=KT)
        v_g = carve(2 * D).rearrange("p (a n) -> p a n", a=2)
        b_mix = carve(KT * P, 1).rearrange("p (g t) -> p g t", g=KT)
        v_sum, v_mean, v_var, v_rt, v_rstd = (carve(2) for _ in range(5))

        bank = [ctx.enter_context(nc.psum_tensor(f"bank{i}", [P, 2 * T], F32)) for i in range(8)]
        GATE, UP, MISC, STAT = 4, 5, 6, 7
        bias_rows = nc.dram_tensor("bias_rows_scratch", [HA, SKEW], F32).ap()
        skew = nc.dram_tensor("skew_scratch", [HA, P, SKEW], F32).ap()

        raw_in = [sem(f"raw_in{i}") for i in range(SLOTS)]
        hi_ready, lo_ready, lo_pool, chunks_done = (sem(s) for s in ("hi_ready", "lo_ready", "lo_pool", "chunks_done"))
        x_in = [sem(f"x_in{i}") for i in range(X_PARTS)]
        x_ready, sq_ready, ss_ready = sem("x_ready"), sem("sq_ready"), sem("ss_ready")
        log_ready, rstd_ready, t_ready = sem("log_ready"), sem("rstd_ready"), sem("t_ready")
        xhi_ready, xs_ready, sq_added = sem("xhi_ready"), sem("xs_ready"), sem("sq_added")
        silu_done, gu_ready, guhi_ready, gulo_ready = (sem(s) for s in ("silu_done", "gu_ready", "guhi_ready", "gulo_ready"))
        bank_done = sem("bank_done")
        ada_in = [sem("ada_in0"), sem("ada_in1")]
        ada_step, ada_summed, ada_stored = sem("ada_step"), sem("ada_summed"), sem("ada_stored")
        cs_t, cs_hi_ready, cs_ready = sem("cs_t"), sem("cs_hi_ready"), sem("cs_ready")
        cols_in, consts_in = sem("cols_in"), sem("consts_in")
        memsets, dve_chain = sem("memsets"), sem("dve_chain")
        out_done = sem("out_done")
        S = {}

        def ev(name):
            if name not in S:
                S[name] = sem(name)
            return S[name]

        block = ctx.enter_context(nc.Block())

        def col(name, i=0):
            at = COLS[name][0] + i
            return cols[:, at:at + 1]

        def pools(c):
            return any(BASE[n] <= c < BASE[n] + POOLED[n] for n in range(len(STAGES)))

        def low_done(c):
            return (lo_pool if pools(c) else lo_ready), sum(pools(b) == pools(c) for b in range(c + 1))

        def modc(layer, m, k, n=1):
            return mod[:, layer, 8 * m + k:8 * m + k + n]

        def norm_cols(n):
            plain = {0: "ffn1_norm", 1: "mix_norm", 2: "ffn2_norm", 3: "ple_norm", 4: "final_norm"}
            if n in plain:
                return (lambda k: col(plain[n], k)), None
            if n in (8, 12):
                return (lambda k: col("ln_out_2", 8 * (n // 12) + k)), None
            layer, j = (0, n - 5) if n < 8 else (1, n - 9)
            return (lambda k: a_col[:, layer, 8 * j + k:8 * j + k + 1]), (lambda k: modc(layer, 3 * j, k))

        def lin(slot, w):
            return w[:, slot, :].rearrange("p (k n) -> p k n", k=KT)

        def tail(slot, w):
            return w[:, slot, :].rearrange("p (j n) -> p j n", j=2)

        MIX_COLS = [512, 0, 768, 256, 1024, 1280, 1536, 1792, 2048, 2304]
        SUB_BANK = [3, 2, 3, 3]

        @block.sync
        def _(sp):
            def load(c, src, i=0):
                s = c % SLOTS
                if c >= SLOTS:
                    done, value = low_done(c - SLOTS)
                    sp.wait_ge(done, value + 3 * i)
                sp.dma_start(raw[:, s, :].rearrange("p (k n) -> p k n", k=src.shape[1]), src)\
                    .then_inc(raw_in[s], 16)

            def over_k(w, at):
                return w[:, bass.ds(at, NC)].rearrange("(k p) n -> p k n", p=P)

            def over_f(w, at):
                return w[bass.ds(at, NC), :].rearrange("(j p) n -> p j n", p=P)

            def load_ada(layer, block_no, half, after):
                if after is not None:
                    sp.wait_ge(ada_step, after + 4 * half + 4)
                src = a["ada_w_2"][layer, half * 512:(half + 1) * 512, bass.ds(block_no * ADA_W, ADA_W)]
                sp.dma_start(ada[:, half, :].rearrange("p (k n) -> p k n", k=4),
                             src.rearrange("(k p) n -> p k n", p=P)).then_inc(ada_in[half], 16)

            def ffn_weights(n):
                f = FFN_NO[n]
                if f < 2:
                    w_in, w_down = a[f"ffn{f + 1}_w_in"][0], a[f"ffn{f + 1}_w_out"][0]
                    return w_in[:, 0:F], w_in[:, F:2 * F], w_down
                layer, j = (f - 2) // 2, f % 2 + 1
                return tuple(a[f"ffn{j}_{w}_2"][layer] for w in ("wg", "wu", "wd"))

            def ffn(n):
                gate, up, down = ffn_weights(n)
                f, c0 = FFN_NO[n], BASE[n]
                load(c0, over_k(gate, 0))
                load(c0 + 1, over_k(up, 0))
                load(c0 + 2, over_k(gate, NC))
                load(c0 + 3, over_k(up, NC))
                load(c0 + 4, over_f(down, 0))
                cl = c0 + 5
                with_ada = f < 4
                layer, first = f // 2, (f % 2) * LOOPED

                def ada_block(i, half):
                    first_of_all = isinstance(i, int) and i == 0 and f == 0
                    load_ada(layer, i + first, half, None if first_of_all else (i + f * LOOPED - 1) * 8)

                def step(i):
                    load(cl, over_k(gate, (i + 2) * NC), i)
                    load(cl + 1, over_k(up, (i + 2) * NC), i)
                    if with_ada:
                        ada_block(i, 0)
                    load(cl + 2, over_f(down, (i + 1) * NC), i)
                    if with_ada:
                        ada_block(i, 1)

                load(cl, over_k(gate, 2 * NC))
                load(cl + 1, over_k(up, 2 * NC))
                load(cl + 2, over_f(down, NC))
                if with_ada:
                    if f > 0:
                        sp.wait_ge(x_ready, 8 * n)
                    for half in range(2):
                        ada_block(0, half)
                with sp.Fori(1, LOOPED) as i:
                    step(i)
                load(c0 + 32, over_f(down, (STEPS - 1) * NC))

            for i in range(X_PARTS):
                k = slice(i * KT // X_PARTS, (i + 1) * KT // X_PARTS)
                sp.dma_start(x[:, k, :], a["x"][:, k, :]).then_inc(x_in[i], 16)
            sp.dma_start(cols[:, :], a["cols"]).then_inc(cols_in, 16)
            for n, (kind, _) in enumerate(STAGES):
                c0 = BASE[n]
                if kind == "ffn":
                    ffn(n)
                elif kind == "mix":
                    for j, at in enumerate(MIX_COLS):
                        load(c0 + j, over_k(a["w_in"][0], at))
                    for j in range(4):
                        load(c0 + 10 + j, over_k(a["w_out"][0], j * NC))
                elif kind == "ple":
                    load(c0, over_f(a["ple_w_proj"][0], 0))
                    for j in range(4):
                        load(c0 + 1 + j, over_k(a["ple_w_gate"][0], j * NC))
                elif kind == "attn":
                    w = a["attn_w_qkv_2"][0]
                    for i in range(4):
                        for part in range(3):
                            load(c0 + 3 * i + part, over_k(w, part * D + i * NC))
                    for j in range(4):
                        load(c0 + 12 + j, over_k(a["attn_w_o_2"][0], j * NC))
                elif kind == "sgu":
                    w = a["sgu_w_in_2"][0]
                    for j in range(4):
                        load(c0 + j, over_k(w, D + j * NC))
                    for j in range(4):
                        load(c0 + 4 + j, over_k(w, j * NC))
                    for j in range(4):
                        load(c0 + 8 + j, over_k(a["sgu_w_out_2"][0], j * NC))
            for k in range(0, KT, KT // X_PARTS):
                sp.wait_ge(x_ready, 8 * (len(STAGES) - 1) + k + KT // X_PARTS)
                sp.dma_start(out[:, k:k + KT // X_PARTS, :], x[:, k:k + KT // X_PARTS, :]).then_inc(out_done, 16)
            sp.wait_ge(out_done, 16 * X_PARTS)

        @block.gpsimd
        def _(pool):
            def lows(n):
                c, count = BASE[n], POOLED[n]

                def low_part(m, i):
                    s = (c + m) % SLOTS
                    pool.wait_ge(hi_ready, c + m + 1 + 3 * i)
                    pool.tensor_tensor(w_lo[:, s, :], raw[:, s, :], w_hi[:, s, :].bitcast(F32), ALU.subtract)\
                        .then_inc(lo_pool, 1)

                if count > SLOTS:
                    with pool.Fori(0, count // SLOTS) as i:
                        for m in range(SLOTS):
                            low_part(m, i)
                for m in range(count % SLOTS):
                    low_part(m, count // SLOTS)

            pool.memset(eps_col[:, :], EPS).then_inc(memsets, 1)
            pool.memset(one_col[:, :], 1.0).then_inc(memsets, 1)
            pool.memset(ones_d[:, :], 1.0 / D).then_inc(memsets, 1)
            pool.memset(ones_c[:, :], 1.0 / (CT * P)).then_inc(memsets, 1)
            pool.memset(ones_v[:, :], 1.0 / P).then_inc(memsets, 1)
            pool.memset(ones_1[:, :], 1.0).then_inc(memsets, 1)
            pool.memset(zero_col[:, :], 0.0).then_inc(memsets, 1)
            pool.wait_ge(memsets, 7)
            pool.memset(table[NB:NB + 1, :], -1e30).then_inc(memsets, 1)
            pool.dma_start(table[0:NB, :], a["rel_bias_2"]).then_inc(ev("table_in"), 16)
            pool.dma_start(one_hot, a["one_hot"]).then_inc(ev("table_in"), 16)
            pool.dma_start(lam_in[:, 0:4], a["lam"]).then_inc(ev("lam_in"), 16)
            pool.dma_start(consts[:, :, :], a["consts"]).then_inc(consts_in, 16)
            pool.wait_ge(ev("rows_copied"), 1)
            pool.dma_start(bias_rows, rows).then_inc(ev("rows_out"), 16)
            pool.wait_ge(ev("rows_out"), 16)
            pool.dma_start(skew, bias_rows.unsqueeze(1).to_broadcast([HA, P, SKEW])).then_inc(ev("skew_out"), 16)
            pool.memset(glu[:, :, 0:CONV - 1], 0.0).then_inc(ev("glu_pad"), 1)
            pool.wait_ge(ev("glu_pad"), 1)
            pool.memset(glr, 1.0).then_inc(ev("glr_ones"), 1)
            pool.wait_ge(ev("glr_ones"), 1)
            pool.dma_start(w_glr, a["w_in"][0][:, 2560:2576].rearrange("(k p) n -> p k n", p=P))\
                .then_inc(ev("gate_w_in"), 16)
            pool.dma_start(wup[0:16, :], a["gate_w_up"][0]).then_inc(ev("gate_w_in"), 16)
            pool.dma_start(wup[16:17, :], a["gate_b"]).then_inc(ev("gate_w_in"), 16)
            for par in range(2):
                pool.memset(score[par], 0.0).then_inc(ev("score_zero"), 1)
                pool.wait_ge(ev("score_zero"), par + 1)
            lows(1)
            lows(2)
            pool.wait_ge(x_ready, 8 * 2)
            pool.dma_start(ub[:, 0:2, :], a["p"]).then_inc(ev("p_in"), 16)
            pool.wait_ge(ev("skew_out"), 16)
            pool.wait_ge(x_ready, 8 * 2)
            skewed = skew.rearrange("h p j -> (h p j)")
            for lo, n, at in ((SKEW - T, T, 0), (0, P, P)):
                src = bass.AP(skewed.tensor, P - 1 + at, [[SKEW - 1, P], [P * SKEW, HA], [1, n]])
                pool.dma_start(bias_t[:, :, (P if n == T else 0):(P if n == T else 0) + n], src)\
                    .then_inc(ev("bias_in"), 16)
            for n in (3, 5, 6, 7):
                lows(n)
            pool.wait_ge(x_ready, 8 * 7)
            pool.dma_start(ln_rows[:, 0, :], a["sgu_ln_g_2"][0:1, :].to_broadcast([P, D])).then_inc(ev("sgu_in"), 16)
            pool.dma_start(ln_rows[:, 1, :], a["sgu_ln_b_2"][0:1, :].to_broadcast([P, D])).then_inc(ev("sgu_in"), 16)
            pool.dma_start(w_mix, a["w_mix"]).then_inc(ev("sgu_in"), 16)
            pool.dma_start(b_mix, a["sgu_b_s_2"]).then_inc(ev("sgu_in"), 16)
            for n in (9, 10, 11):
                lows(n)

        @block.scalar
        def _(act):
            def split(c, s=None):
                looped = s is not None
                if not looped and c >= TOTAL:
                    return
                s = c % SLOTS if s is None else s
                if looped:
                    act.wait_ge(raw_in[s], (c[0] // SLOTS + 1) * 16 + c[1] * 16)
                    act.wait_ge(chunks_done, c[0] - SLOTS + 1 + c[1] * 3)
                else:
                    act.wait_ge(raw_in[s], 16 * (c // SLOTS + 1))
                    if c >= SLOTS:
                        act.wait_ge(chunks_done, c - SLOTS + 1)
                act.activation(w_hi[:, s, :], raw[:, s, :], ACT.Copy).then_inc(hi_ready, 1)

            def norm(n):
                kind = STAGES[n][0]
                for k in range(KT):
                    if n == 0:
                        act.wait_ge(x_in[k * X_PARTS // KT], 16)
                    else:
                        act.wait_ge(x_ready, 8 * (n - 1) + k + 1)
                    act.activation(xn[:, k, :], x[:, k, :], ACT.Square).then_inc(sq_ready, 1)
                if n == 0:
                    split(0)
                act.preload_act_table_set(LN_EXP)
                act.wait_ge(ss_ready, n + 1)
                act.activation(rstd[:, 0:T], bank[STAT][:, 0:T], ACT.Ln, bias=eps_col[:, :]).then_inc(log_ready, 1)
                act.wait_ge(log_ready, n + 1)
                act.activation(rstd[:, 0:T], rstd[:, 0:T], ACT.Exp, scale=-0.5).then_inc(rstd_ready, 1)
                if kind == "renorm":
                    return
                shift = norm_cols(n)[1]
                for k in range(KT):
                    act.wait_ge(t_ready, 8 * SPLIT_NO[n] + k + 1)
                    if shift is None:
                        act.activation(xs_hi[:, k, :], xn[:, k, :], ACT.Copy).then_inc(xhi_ready, 1)
                    else:
                        act.activation(xs_hi[:, k, :], xn[:, k, :], ACT.Identity, bias=shift(k)).then_inc(xhi_ready, 1)
                if n == 0:
                    split(1)

            def ffn(n):
                f, c0 = FFN_NO[n], BASE[n]
                s0 = STEPS * f
                if n == 0:
                    act.wait_ge(cols_in, 16)

                def silu(s, c):
                    act.wait_ge(chunks_done, c + 1)
                    act.activation(silu_g[:, :], bank[GATE][:, :], ACT.Silu).then_inc(silu_done, 1)

                def gu_high(s, c):
                    act.wait_ge(gu_ready, s0 + s + 1)
                    if c is not None:
                        act.wait_ge(chunks_done, c + 1)
                    out_hi = last_hi if isinstance(s, int) and s == STEPS - 1 else gu_hi[:, :]
                    act.activation(out_hi, gu[:, :], ACT.Copy).then_inc(guhi_ready, 1)

                split(c0 + 2)
                silu(0, c0)
                if n == 0:
                    act.activation(c_act[:, :], cols[:, COLS["c_2"][0]:COLS["c_2"][0] + KT], ACT.Silu)\
                        .then_inc(ev("c_act"), 1)
                    act.wait_ge(ev("lam_sum"), 1)
                    act.wait_ge(ev("rows_copied"), 1)
                    act.activation(lam_e[:, :], bank[MISC][:, SKEW:SKEW + 2], ACT.Exp).then_inc(ev("lam_exp"), 1)
                split(c0 + 3)
                gu_high(0, None)
                split(c0 + 4)
                silu(1, c0 + 2)
                split(c0 + 5)
                cl = c0 + 5
                with act.Fori(0, LOOPED) as i:
                    split((cl + 1, i), (cl + 1) % SLOTS)
                    gu_high(i + 1, cl + 3 * i - 1)
                    split((cl + 2, i), (cl + 2) % SLOTS)
                    silu(i + 2, cl + 3 * i)
                    split((cl + 3, i), (cl + 3) % SLOTS)
                gu_high(STEPS - 1, None)
                split(c0 + 33)
                split(c0 + 34)

            def mix(n):
                c = BASE[n]
                split(c + 2)
                split(c + 3)
                for pair, s in ((0, c + 4), (1, c + 6)):
                    act.wait_ge(chunks_done, c + 2 * pair + 1)
                    if pair:
                        act.wait_ge(ev("glu_done"), 1)
                    act.activation(silu_g[:, :], bank[1 + 2 * pair][:, :], ACT.Sigmoid).then_inc(ev("conv_sig"), 1)
                    split(s)
                    if not pair:
                        split(c + 5)
                act.wait_ge(chunks_done, c + 5)
                act.wait_ge(ev("rows_out"), 16)
                act.activation(q_s, bank[4][:, :], ACT.Copy, scale=HEAD_SCALE).then_inc(ev("qk_copied"), 1)
                split(c + 7)
                act.wait_ge(chunks_done, c + 6)
                act.activation(k_s, bank[5][:, :], ACT.Copy).then_inc(ev("qk_copied"), 1)
                act.wait_ge(ev("glr_done"), 1)
                act.wait_ge(ev("glr_ones"), 1)
                act.activation(glr[0:16, :], bank[MISC][0:16, 0:T], ACT.Copy).then_inc(ev("glr_copied"), 1)
                split(c + 8)
                act.wait_ge(chunks_done, c + 7)
                act.activation(v_tok[:, 0, :, :], bank[0][:, :].rearrange("p (a n) -> p a n", a=2), ACT.Copy)\
                    .then_inc(ev("v_copied"), 1)
                act.wait_ge(ev("z_done"), 1)
                act.preload_act_table_set(LN_EXP)
                act.activation(e_pos, bank[STAT][:, :], ACT.Abs).then_inc(ev("la_act"), 1)
                act.wait_ge(ev("la_act"), 1)
                act.activation(e_neg, e_pos, ACT.Exp, scale=-1.0).then_inc(ev("la_act"), 1)
                act.wait_ge(ev("la_act"), 2)
                act.activation(e_pos, e_neg, ACT.Ln, bias=one_col[:, :]).then_inc(ev("la_act"), 1)
                split(c + 9)
                act.wait_ge(chunks_done, c + 8)
                act.activation(v_tok[:, 1, :, :], bank[1][:, :].rearrange("p (a n) -> p a n", a=2), ACT.Copy)\
                    .then_inc(ev("v_copied"), 1)
                act.wait_ge(ev("cum_done"), 1)
                act.activation(e_pos, bank[MISC][:, :], ACT.Exp).then_inc(ev("e_done"), 1)
                act.activation(e_neg, bank[MISC][:, :], ACT.Exp, scale=-1.0).then_inc(ev("e_done"), 1)
                split(c + 10)
                act.wait_ge(ev("cum_end"), 1)
                for i in range(8):
                    act.activation(k_exp[:, i * CHUNK:(i + 1) * CHUNK], bank[MISC][:, i * CHUNK:(i + 1) * CHUNK],
                                   ACT.Exp, scale=-1.0, bias=cum_end[:, i:i + 1]).then_inc(ev("k_exp"), 1)
                act.activation(decay, cum_end, ACT.Exp).then_inc(ev("decay"), 1)
                for m in range(2):
                    act.wait_ge(chunks_done, c + 9 + m)
                    act.activation(silu_r[:, 2 * m:2 * m + 2, :], bank[2 + m][:, :].rearrange("p (a n) -> p a n", a=2),
                                   ACT.Silu).then_inc(ev("silu_r"), 1)
                    split(c + 11 + m)
                act.preload_act_table_set(LN_EXP)
                act.wait_ge(ev("ke_turned"), 1)
                act.activation(ke_t, bank[STAT][:, :].rearrange("p (a n) -> p a n", a=2), ACT.Copy)\
                    .then_inc(ev("ke_copied"), 1)
                for par in range(2):
                    act.wait_ge(ev("o_done"), par + 1)
                    act.activation(ub[:, 4 + 2 * par:6 + 2 * par, :], bank[6 + par][:, :].rearrange("p (a n) -> p a n", a=2),
                                   ACT.Square).then_inc(ev("o_sq"), 1)
                for par, r in enumerate(o_rstd):
                    act.wait_ge(ev("o_ms"), par + 1)
                    act.activation(r, bank[4 + par][:, :], ACT.Ln, bias=eps_col[:, :]).then_inc(ev("o_log"), 1)
                    act.wait_ge(ev("o_log"), par + 1)
                    act.activation(r, r, ACT.Exp, scale=-0.5).then_inc(ev("o_rstd"), 1)
                for h in range(HG):
                    act.wait_ge(cs_t, h + 1)
                    act.activation(cs_hi[:, 4 + h, :], xn[:, 4 + h, :], ACT.Copy).then_inc(cs_hi_ready, 1)
                act.wait_ge(ev("ln_centred"), 1)
                act.activation(conv_y, ub[:, 0:4, :], ACT.Square).then_inc(ev("ln_sq"), 1)
                act.wait_ge(ev("ln_var"), 1)
                act.activation(ln_rstd_s, bank[3][:, T:2 * T], ACT.Ln, bias=eps_col[:, :]).then_inc(ev("ln_log"), 1)
                act.wait_ge(ev("ln_log"), 1)
                act.activation(ln_rstd_s, ln_rstd_s, ACT.Exp, scale=-0.5).then_inc(ev("ln_rstd"), 1)
                for k in range(CT):
                    act.wait_ge(ev("ln_t"), k + 1)
                    act.activation(xn[:, k, :], conv_y[:, k, :], ACT.Silu, scale=col("conv_ln_g", k),
                                   bias=col("conv_ln_b", k)).then_inc(ev("ln_silu"), 1)
                for k in range(CT):
                    act.wait_ge(ev("ln_silu"), k + 1)
                    act.activation(cs_hi[:, k, :], xn[:, k, :], ACT.Copy).then_inc(cs_hi_ready, 1)
                for j in range(1, 4):
                    split(c + 12 + j)

            def ple(n):
                c = BASE[n]
                act.wait_ge(ev("p_in"), 16)
                act.activation(cs_hi[:, 0:2, :], ub[:, 0:2, :], ACT.Copy).then_inc(ev("p_hi"), 1)
                norm(n)
                split(c + 2)
                split(c + 3)
                for j in range(4):
                    act.wait_ge(chunks_done, c + 2 + j)
                    if j:
                        act.wait_ge(ev("ple_mul"), j)
                    act.activation(silu_g[:, :], bank[4 + j % 2][:, :], ACT.Sigmoid).then_inc(ev("ple_sig"), 1)
                    if j < 3:
                        split(c + 4 + j)

            def attention(n):
                c = BASE[n]

                def heads(i, j):
                    e = 2 * i + j
                    for m in range(4):
                        comp, part = m % 2, m // 2
                        act.wait_ge(ev("peak"), 2 * e + part + 1)
                        seg = logit[:, comp, (P if part else 0):(SKEW if part else P)]
                        act.activation(seg, seg, ACT.Exp, bias=peak[:, m:m + 1],
                                       accum_out=total[:, m:m + 1]).then_inc(ev("exp"), 1)

                def turned(i, j):
                    e = 2 * i + j
                    act.wait_ge(ev("turned"), e + 1)
                    act.activation(attn_t, bank[MISC][:, 0:SKEW], ACT.Copy).then_inc(ev("turned_copied"), 1)

                def outs(i):
                    act.wait_ge(ev("pair_done"), i + 1)
                    act.activation(xn[:, bass.ds(2 * i, 2), :] , bank[7][:, :].rearrange("p (a n) -> p a n", a=2),
                                   ACT.Copy).then_inc(ev("o_copied"), 1)

                def qk_in(i, which):
                    act.wait_ge(chunks_done, c + 3 * i + which + 1)
                    if which:
                        act.wait_ge(ev("qk_norm_ms"), 2 * i + 1)
                    act.activation((q_raw, k_raw)[which], bank[which][:, :], ACT.Copy).then_inc(ev("qk_raw"), 1)
                    act.activation(qk_sq, bank[which][:, :], ACT.Square).then_inc(ev("qk_sq"), 1)

                def qk_root(i, which):
                    act.wait_ge(ev("qk_norm_ms"), 2 * i + which + 1)
                    if which or not isinstance(i, int):
                        act.wait_ge(ev("qk_n"), 2 * i + which)
                    act.activation(rstd[:, :], bank[3][:, :], ACT.Ln, bias=eps_col[:, :]).then_inc(ev("qk_log"), 1)
                    act.wait_ge(ev("qk_log"), 2 * i + which + 1)
                    act.activation(rstd[:, :], rstd[:, :], ACT.Exp, scale=-0.5).then_inc(ev("qk_rstd"), 1)

                def values(i):
                    act.wait_ge(chunks_done, c + 3 * i + 3)
                    act.activation(va, bank[2][:, :].rearrange("p (a n) -> p a n", a=2), ACT.Copy)\
                        .then_inc(ev("va"), 1)

                def pair(i, c_at, before):
                    def sp_(m):
                        if isinstance(i, int):
                            split(c + 3 * i + m)
                        else:
                            split((c + 3 + m, i - 1), (c + 3 + m) % SLOTS)
                    sp_(2)
                    qk_in(i, 0)
                    sp_(3)
                    if before:
                        heads(i - 1, 0)
                    qk_root(i, 0)
                    qk_in(i, 1)
                    sp_(4)
                    if before:
                        turned(i - 1, 0)
                        heads(i - 1, 1)
                        turned(i - 1, 1)
                        outs(i - 1)
                    qk_root(i, 1)
                    values(i)

                def sub_squares(j):
                    act.wait_ge(ev("o_copied"), j + 1)
                    act.activation(ub[:, 2 * j:2 * j + 2, :], xn[:, 2 * j:2 * j + 2, :], ACT.Square)\
                        .then_inc(ev("sub_sq"), 1)

                def sub_root(j):
                    act.wait_ge(ev("sub_ms"), j + 1)
                    act.activation(sub_rstd[j], bank[SUB_BANK[j]][:, :], ACT.Ln, bias=eps_sub[:, :]).then_inc(ev("sub_log"), 1)
                    act.wait_ge(ev("sub_log"), j + 1)
                    act.activation(sub_rstd[j], sub_rstd[j], ACT.Exp, scale=-0.5).then_inc(ev("sub_rstd"), 1)

                def highs(ks):
                    for k in ks:
                        act.wait_ge(cs_t, 4 + k + 1)
                        act.activation(cs_hi[:, k, :], ub[:, k, :], ACT.Copy).then_inc(cs_hi_ready, 1)

                pair(0, c, False)
                with act.Fori(1, 4) as i:
                    pair(i, None, True)
                for j in range(3):
                    sub_squares(j)
                split(c + 14)
                sub_root(0)
                heads(3, 0)
                sub_root(1)
                turned(3, 0)
                heads(3, 1)
                sub_root(2)
                highs(range(4))
                turned(3, 1)
                outs(3)
                sub_squares(3)
                highs(range(4, 6))
                sub_root(3)
                highs(range(6, 8))
                split(c + 15)
                split(c + 16)
                split(c + 17)

            def gating(n):
                c = BASE[n]
                split(c + 2)
                for j in range(4):
                    if j:
                        split(c + 2 + j)
                    act.wait_ge(chunks_done, c + j + 1)
                    act.activation(v_g[:, :, j * NC:(j + 1) * NC], bank[j][:, :].rearrange("p (a n) -> p a n", a=2),
                                   ACT.Gelu).then_inc(ev("v_gelu"), 1)
                split(c + 6)
                for j in range(4):
                    act.wait_ge(chunks_done, c + 5 + j)
                    act.activation(ub[:, 2 * j:2 * j + 2, :], bank[4 + j % 2][:, :].rearrange("p (a n) -> p a n", a=2),
                                   ACT.Gelu).then_inc(ev("u_gelu"), 1)
                    if j == 0:
                        for t in range(2):
                            act.wait_ge(ev("v_centred"), 2)
                            act.activation(xn[:, 0:4, :] if t == 0 else xn[:, 4:8, :],
                                           v_g[:, t, :].rearrange("p (a n) -> p a n", a=4), ACT.Square,
                                           accum_out=v_var[:, t:t + 1]).then_inc(ev("v_sq"), 1)
                        act.wait_ge(ev("v_sq"), 2)
                        act.activation(v_rt, v_var, ACT.Sqrt, scale=1.0 / D, bias=eps_col[:, :]).then_inc(ev("v_rt"), 1)
                    if j < 3:
                        split(c + 7 + j)
                split(c + 10)
                for k in range(KT):
                    act.wait_ge(cs_t, 12 + k + 1)
                    act.activation(cs_hi[:, k, :], xn[:, k, :], ACT.Copy).then_inc(cs_hi_ready, 1)
                split(c + 11)
                split(c + 12)
                split(c + 13)

            act.wait_ge(memsets, 8)
            for n, (kind, _) in enumerate(STAGES):
                if kind != "ple":
                    norm(n)
                {"ffn": ffn, "mix": mix, "ple": ple, "attn": attention, "sgu": gating, "renorm": lambda n: None}[kind](n)

        @block.vector
        def _(dve):
            chain = [0]

            def link(ins):
                chain[0] += 1
                ins.then_inc(dve_chain, 1)
                dve.wait_ge(dve_chain, chain[0])

            def split(c, s=None):
                looped = s is not None
                if not looped and (c >= TOTAL or pools(c)):
                    return
                if looped:
                    dve.wait_ge(hi_ready, c[0] + 1 + 3 * c[1])
                else:
                    s = c % SLOTS
                    dve.wait_ge(hi_ready, c + 1)
                dve.tensor_tensor(w_lo[:, s, :], raw[:, s, :], w_hi[:, s, :].bitcast(F32), ALU.subtract)\
                    .then_inc(lo_ready, 1)

            def low(out_lo, t, hi, shift=None):
                if shift is None:
                    return dve.tensor_tensor(out_lo, t, hi.bitcast(F32), ALU.subtract)
                return dve.scalar_tensor_tensor(out=out_lo, in0=t, scalar=shift, in1=hi.bitcast(F32),
                                                op0=ALU.add, op1=ALU.subtract)

            def norm(n):
                scale, shift = norm_cols(n)
                if n == 0:
                    dve.wait_ge(cols_in, 16)
                    split(0)
                dve.wait_ge(rstd_ready, n + 1)
                if STAGES[n][0] == "renorm":
                    for k in range(KT):
                        dve.scalar_tensor_tensor(out=x[:, k, :], in0=x[:, k, :], scalar=scale(k), in1=rstd[:, 0:T],
                                                 op0=ALU.mult, op1=ALU.mult).then_inc(x_ready, 1)
                    return
                s = 8 * SPLIT_NO[n]

                def lower(k):
                    dve.wait_ge(xhi_ready, s + k + 1)
                    low(xs_lo[:, k, :], xn[:, k, :], xs_hi[:, k, :], shift and shift(k)).then_inc(xs_ready, 1)

                for k in range(KT):
                    dve.scalar_tensor_tensor(out=xn[:, k, :], in0=x[:, k, :], scalar=scale(k), in1=rstd[:, 0:T],
                                             op0=ALU.mult, op1=ALU.mult).then_inc(t_ready, 1)
                    if k:
                        lower(k - 1)
                lower(KT - 1)
                if n == 0:
                    split(1)

            def ffn(n):
                f, c0 = FFN_NO[n], BASE[n]
                s0 = STEPS * f
                layer, first = f // 2, (f % 2) * LOOPED

                def gu_mul(s, c):
                    dve.wait_ge(chunks_done, c + 1)
                    dve.wait_ge(silu_done, s0 + s + 1)
                    if not (isinstance(s, int) and s0 + s == 0):
                        dve.wait_ge(gulo_ready, s0 + s)
                    dve.tensor_tensor(gu[:, :], bank[UP][:, :], silu_g[:, :], ALU.mult).then_inc(gu_ready, 1)

                def gu_low(s):
                    dve.wait_ge(guhi_ready, s0 + s + 1)
                    last = isinstance(s, int) and s == STEPS - 1
                    low(last_lo if last else gu_lo[:, :], gu[:, :], last_hi if last else gu_hi[:, :])\
                        .then_inc(gulo_ready, 1)

                def ada_half(i, half):
                    done = 8 * LOOPED * f + 8 * i
                    dve.wait_ge(ada_in[half], 16 * (i + LOOPED * f) + 16)
                    if f == 0 and half == 0:
                        dve.wait_ge(ev("c_act"), 1)
                    for m in range(4):
                        k = 4 * half + m
                        w = ada[:, half, m * ADA_W:(m + 1) * ADA_W]
                        if k == 0:
                            dve.tensor_scalar(ada_acc[:, :], w, c_act[:, 0:1], None, ALU.mult).then_inc(ada_step, 1)
                        else:
                            dve.wait_ge(ada_step, done + k)
                            dve.scalar_tensor_tensor(out=ada_acc[:, :], in0=w, scalar=c_act[:, k:k + 1],
                                                     in1=ada_acc[:, :], op0=ALU.mult, op1=ALU.add)\
                                .then_inc(ada_step, 1)

                def ada_store(i):
                    at = (i + first) * 4
                    dve.wait_ge(ada_summed, i + LOOPED * f + 1)
                    dve.tensor_tensor(mod[:, layer, bass.ds(at, 4)], bank[MISC][:, 0:4],
                                      cols[:, bass.ds(at + COLS["ada_b_2"][0] + 72 * layer, 4)], ALU.add)\
                        .then_inc(ada_stored, 1)

                if n == 0:
                    dve.wait_ge(ev("lam_in"), 16)
                    dve.tensor_tensor(lam_in[:, 4:6], lam_in[:, 0:4:2], lam_in[:, 1:4:2], ALU.mult)\
                        .then_inc(ev("lam_prod"), 1)
                split(c0 + 2)
                if n == 0:
                    attention_constants()
                split(c0 + 3)
                gu_mul(0, c0 + 1)
                gu_low(0)
                split(c0 + 4)
                split(c0 + 5)
                gu_mul(1, c0 + 3)
                cl = c0 + 5
                with dve.Fori(0, LOOPED) as i:
                    split((cl + 1, i), (cl + 1) % SLOTS)
                    gu_low(i + 1)
                    if f < 4:
                        ada_half(i, 0)
                    split((cl + 2, i), (cl + 2) % SLOTS)
                    if f < 4:
                        ada_half(i, 1)
                    split((cl + 3, i), (cl + 3) % SLOTS)
                    gu_mul(i + 2, cl + 3 * i + 1)
                    if f < 4:
                        ada_store(i)
                gu_low(STEPS - 1)
                split(c0 + 33)
                split(c0 + 34)
                residual(n, lambda b: (bank_done, 3 * f + b + 1) if b < 3 else (chunks_done, c0 + 33))

            def attention_constants():
                dve.wait_ge(ev("rows_mm"), 1)
                dve.tensor_copy(rows, bank[MISC][0:HA, 0:SKEW]).then_inc(ev("rows_copied"), 1)
                dve.wait_ge(ev("lam_exp"), 1)
                link(dve.tensor_tensor(nlam[:, :], lam_e[:, 1:2], lam_e[:, 0:1], ALU.subtract))
                link(dve.tensor_scalar(nlam[:, :], nlam[:, :], -LAMBDA_INIT, None, ALU.add))
                link(dve.scalar_tensor_tensor(out=lam_size[:, :], in0=nlam[:, :], scalar=-1.0, in1=nlam[:, :],
                                              op0=ALU.mult, op1=ALU.max))
                link(dve.tensor_scalar(lam_size[:, :], lam_size[:, :], 1.0, None, ALU.max))
                link(dve.reciprocal(lam_r[:, :], lam_size[:, :]))
                for i in range(2):
                    link(dve.tensor_copy(lam_coef[:, 2 * i:2 * i + 1], lam_r[:, :]))
                    link(dve.tensor_tensor(lam_coef[:, 2 * i + 1:2 * i + 2], lam_r[:, :], nlam[:, :], ALU.mult))
                link(dve.tensor_tensor(eps_sub[:, :], lam_r[:, :], lam_r[:, :], ALU.mult))
                link(dve.tensor_scalar(eps_sub[:, :], eps_sub[:, :], EPS, TINY, ALU.mult, ALU.max))
                link(dve.tensor_scalar(ms_limit[:, :], lam_r[:, :], FLT_MAX / P, lam_r[:, :], ALU.mult, ALU.mult))
                link(dve.tensor_scalar(sub_g[:, :], col("attn_subln_2"), 1.0 - LAMBDA_INIT, None, ALU.mult))

            def add_squares(n, b):
                if n < len(STAGES):
                    dve.wait_ge(sq_ready, 8 * n + 2 * b + 2)
                    dve.tensor_tensor(xn[:, 2 * b, :], xn[:, 2 * b, :], xn[:, 2 * b + 1, :], ALU.add)\
                        .then_inc(sq_added, 1)

            def residual(n, done):
                kind = STAGES[n][0]
                layer, j = (0, n - 5) if n < 8 else (1, n - 9)
                for k in range(KT):
                    if k % 2 == 0:
                        dve.wait_ge(*done(k // 2))
                    src = bank[k // 2][:, (k % 2) * T:(k % 2 + 1) * T]
                    if n < 5:
                        factor = 0.5 if kind == "ffn" else 1.0
                    elif kind == "ffn":
                        factor = half_g[:, layer, 8 * (j // 2) + k:8 * (j // 2) + k + 1]
                    else:
                        factor = modc(layer, 5, k)
                    dve.scalar_tensor_tensor(out=x[:, k, :], in0=src, scalar=factor, in1=x[:, k, :],
                                             op0=ALU.mult, op1=ALU.add).then_inc(x_ready, 1)
                    if k % 2 == 0 and k > 1:
                        add_squares(n + 1, k // 2 - 1)

            def projected(n, c):
                residual(n, lambda b: (chunks_done, c + b + 1))

            def modulation(layer):
                dve.wait_ge(ada_stored, ADA_BLOCKS * (layer + 1))
                for j, g in enumerate(("ln_ffn1_2", "ln_mix_2", "ln_ffn2_2")):
                    at = COLS[g][0] + 8 * layer
                    link(dve.scalar_tensor_tensor(out=a_col[:, layer, 8 * j:8 * j + 8],
                                                  in0=modc(layer, 3 * j + 1, 0, 8), scalar=one_col[:, :],
                                                  in1=cols[:, at:at + 8], op0=ALU.add, op1=ALU.mult))
                for j in range(2):
                    link(dve.tensor_scalar(half_g[:, layer, 8 * j:8 * j + 8], modc(layer, 6 * j + 2, 0, 8),
                                           0.5, None, ALU.mult))

            conv_step = [0]

            def conv(count):
                for _ in range(count):
                    i = conv_step[0]
                    if i >= CT * CONV:
                        return
                    pair, j, k = i // (2 * CONV), (i % (2 * CONV)) // 2, i % 2
                    k += 2 * pair
                    src = glu[:, k, j:j + T]
                    w = col("conv_w", k * CONV + j)
                    if j == 0:
                        dve.wait_ge(ev("glu_done"), pair + 1)
                        ins = dve.tensor_scalar(conv_y[:, k, :], src, w, col("conv_b", k), ALU.mult, ALU.add)
                    else:
                        dve.wait_ge(ev("conv_step"), i - 1)
                        ins = dve.scalar_tensor_tensor(out=conv_y[:, k, :], in0=src, scalar=w, in1=conv_y[:, k, :],
                                                       op0=ALU.mult, op1=ALU.add)
                    ins.then_inc(ev("conv_step"), 1)
                    conv_step[0] += 1

            def mix(n):
                c = BASE[n]
                split(c + 2)
                split(c + 3)

                def gated(pair):
                    dve.wait_ge(ev("glu_pad"), 1)
                    dve.wait_ge(ev("conv_sig"), pair + 1)
                    dve.wait_ge(chunks_done, c + 2 * pair + 2)
                    dve.tensor_tensor(glu[:, 2 * pair:2 * pair + 2, CONV - 1:],
                                      bank[2 * pair][:, :].rearrange("p (a n) -> p a n", a=2),
                                      silu_g[:, :].rearrange("p (a n) -> p a n", a=2), ALU.mult)\
                        .then_inc(ev("glu_done"), 1)

                gated(0)
                conv(24)
                gated(1)
                conv(56)
                dve.wait_ge(ev("la_act"), 3)
                dve.scalar_tensor_tensor(out=log_a, in0=bank[STAT][:, :], scalar=zero_col[:, :], in1=e_pos,
                                         op0=ALU.min, op1=ALU.subtract).then_inc(ev("log_a"), 1)
                conv(10)
                dve.wait_ge(ev("e_done"), 2)
                dve.tensor_copy(cum_end, bank[MISC][:, :].rearrange("p (i t) -> p i t", t=CHUNK)[:, :, CHUNK - 1])\
                    .then_inc(ev("cum_end"), 1)
                dve.wait_ge(ev("qk_copied"), 2)
                for o, i0, i1 in ((q_dec, q_s, e_pos), (k_neg, k_s, e_neg), (q_neg, q_s, e_neg), (k_pos, k_s, e_pos)):
                    dve.tensor_tensor(o, i0, i1, ALU.mult).then_inc(ev("qk_scaled"), 1)
                conv(4)
                dve.wait_ge(ev("k_exp"), 8)
                dve.tensor_tensor(k_end, k_s, k_exp, ALU.mult).then_inc(ev("k_end"), 1)
                conv(16)
                dve.wait_ge(consts_in, 16)
                for par in range(2):
                    dve.wait_ge(ev("scored"), par + 1)
                    dve.wait_ge(ev("score_zero"), 2)
                    for i, (m, b) in enumerate(((low_mask, 4 + par), (up_mask, 2 + par))):
                        if i:
                            dve.wait_ge(ev("score_sel"), 2 * par + 1)
                        dve.copy_predicated(score[par], m.bitcast(I32).unsqueeze(1).to_broadcast([P, 4, P]),
                                            bank[b][:, :].rearrange("p (n t) -> p n t", n=4)).then_inc(ev("score_sel"), 1)
                dve.wait_ge(ev("kv_done"), 1)
                dve.wait_ge(ev("decay"), 1)
                dve.tensor_copy(state[:, 0, :, :], bank[0][:, 0:T].rearrange("p (h v) -> p h v", h=2))\
                    .then_inc(ev("state"), 1)
                for i, src in ((1, bank[1][:, 0:T]), (2, bank[0][:, T:2 * T])):
                    for h in range(2):
                        dve.wait_ge(ev("state"), 2 * i - 1)
                        dve.scalar_tensor_tensor(out=state[:, i, h, :], in0=state[:, i - 1, h, :],
                                                 scalar=decay[:, 4 * h + i:4 * h + i + 1],
                                                 in1=src[:, h * P:(h + 1) * P], op0=ALU.mult, op1=ALU.add)\
                            .then_inc(ev("state"), 1)
                conv(CT * CONV)
                for par, r in enumerate(o_rstd):
                    dve.wait_ge(ev("o_rstd"), par + 1)
                    for hh in range(2):
                        h = 2 * hh + par
                        dve.scalar_tensor_tensor(out=xn[:, 4 + h, :], in0=bank[6 + par][:, hh * T:(hh + 1) * T],
                                                 scalar=col("gla_norm", h), in1=r[:, hh * T:(hh + 1) * T],
                                                 op0=ALU.mult, op1=ALU.mult).then_inc(ev("o_normed"), 1)
                dve.wait_ge(ev("silu_r"), 2)
                dve.wait_ge(ev("o_normed"), 4)
                for h in range(HG):
                    dve.tensor_tensor(xn[:, 4 + h, :], xn[:, 4 + h, :], silu_r[:, h, :], ALU.mult).then_inc(cs_t, 1)
                for h in range(HG):
                    dve.wait_ge(cs_hi_ready, h + 1)
                    low(cs_lo[:, 4 + h, :], xn[:, 4 + h, :], cs_hi[:, 4 + h, :]).then_inc(cs_ready, 1)
                dve.wait_ge(ev("ln_mean"), 1)
                dve.tensor_copy(ln_mean_s, bank[3][:, 0:T]).then_inc(ev("ln_mean_copied"), 1)
                dve.wait_ge(ev("ln_mean_copied"), 1)
                dve.tensor_tensor(ub[:, 0:4, :], conv_y, ln_mean_s.unsqueeze(1).to_broadcast([P, 4, T]), ALU.subtract)\
                    .then_inc(ev("ln_centred"), 1)
                dve.wait_ge(ev("ln_rstd"), 1)
                dve.wait_ge(ev("ln_sq"), 1)
                dve.wait_ge(ev("ln_var"), 1)
                for k in range(CT):
                    dve.tensor_tensor(conv_y[:, k, :], ub[:, k, :], ln_rstd_s, ALU.mult).then_inc(ev("ln_t"), 1)
                for k in range(CT):
                    dve.wait_ge(cs_hi_ready, 4 + k + 1)
                    low(cs_lo[:, k, :], xn[:, k, :], cs_hi[:, k, :]).then_inc(cs_ready, 1)
                split(c + 13)
                projected(n, c + 10)

            def ple(n):
                c = BASE[n]
                dve.wait_ge(ev("p_hi"), 1)
                low(cs_lo[:, 0:2, :], ub[:, 0:2, :], cs_hi[:, 0:2, :]).then_inc(ev("p_lo"), 1)
                norm(n)
                split(c + 2)
                split(c + 3)
                for j in range(4):
                    dve.wait_ge(ev("ple_sig"), j + 1)
                    if j:
                        dve.wait_ge(x_ready, 8 * n + 2 * j)
                    dve.tensor_tensor(gu[:, :], bank[j][:, :], silu_g[:, :], ALU.mult).then_inc(ev("ple_mul"), 1)
                    dve.wait_ge(ev("ple_mul"), j + 1)
                    for k in (2 * j, 2 * j + 1):
                        dve.tensor_tensor(x[:, k, :], x[:, k, :], gu[:, (k % 2) * T:(k % 2 + 1) * T], ALU.add)\
                            .then_inc(x_ready, 1)
                    if j < 3:
                        split(c + 4 + j)

            def attention(n):
                c = BASE[n]

                def scored(i, j):
                    e = 2 * i + j
                    if not (isinstance(i, int) and i == 0 and j == 0):
                        dve.wait_ge(ev("attn"), 2 * e)
                    for comp in range(2):
                        dve.wait_ge(ev("logits"), e + 1)
                        dve.scalar_tensor_tensor(out=logit[:, comp, :], in0=bank[4 + comp][:, 0:SKEW], scalar=HEAD_SCALE,
                                                 in1=bias_t[:, bass.ds(2 * i + j, 1), :].rearrange("p a j -> p (a j)"),
                                                 op0=ALU.mult, op1=ALU.add).then_inc(ev("logit"), 1)
                    dve.wait_ge(ev("logit"), 2 * e + 2)
                    for part in range(2):
                        dve.tensor_reduce(peak[:, 2 * part:2 * part + 2],
                                          logit[:, :, (P if part else 0):(SKEW if part else P)], AX_X, ALU.max,
                                          negate=True).then_inc(ev("peak"), 1)

                def weights(i, j):
                    e = 2 * i + j
                    dve.wait_ge(ev("exp"), 4 * e + 4)
                    dve.reciprocal(recip, total).then_inc(ev("recip"), 1)
                    dve.wait_ge(ev("recip"), e + 1)
                    dve.tensor_tensor(coef, recip, lam_coef[:, :], ALU.mult).then_inc(ev("coef"), 1)
                    dve.wait_ge(ev("coef"), e + 1)
                    for part in range(2):
                        seg = slice(P, SKEW) if part else slice(0, P)
                        dve.tensor_scalar(logit[:, 1, seg], logit[:, 1, seg], coef[:, 2 * part + 1:2 * part + 2],
                                          None, ALU.mult).then_inc(ev("p1"), 1)
                    for part in range(2):
                        seg = slice(P, SKEW) if part else slice(0, P)
                        dve.wait_ge(ev("p1"), 2 * e + 1 + part)
                        if part == 0 and not (isinstance(i, int) and i == 0 and j == 0):
                            dve.wait_ge(ev("turned"), e)
                        dve.scalar_tensor_tensor(out=attn[:, seg], in0=logit[:, 0, seg],
                                                 scalar=coef[:, 2 * part:2 * part + 1], in1=logit[:, 1, seg],
                                                 op0=ALU.mult, op1=ALU.add).then_inc(ev("attn"), 1)

                def qk_out(i, which):
                    dve.wait_ge(ev("qk_rstd"), 2 * i + which + 1)
                    dve.scalar_tensor_tensor(out=(q_n, k_n)[which], in0=(q_raw, k_raw)[which],
                                             scalar=col(("attn_q_norm_2", "attn_k_norm_2")[which]), in1=rstd[:, :],
                                             op0=ALU.mult, op1=ALU.mult).then_inc(ev("qk_n"), 1)

                def pair(i, before):
                    if before:
                        scored(i - 1, 0)
                        weights(i - 1, 0)
                        scored(i - 1, 1)
                    qk_out(i, 0)
                    if before:
                        weights(i - 1, 1)
                    qk_out(i, 1)

                def sub_norm(j):
                    dve.wait_ge(ev("sub_rstd"), j + 1)
                    dve.scalar_tensor_tensor(out=sub_rstd[j], in0=bank[SUB_BANK[j]][:, :], scalar=ms_limit[:, :], in1=sub_rstd[j],
                                             op0=ALU.is_le, op1=ALU.mult).then_inc(ev("sub_kept"), 1)
                    dve.wait_ge(ev("sub_kept"), j + 1)
                    for k in (2 * j, 2 * j + 1):
                        dve.scalar_tensor_tensor(out=ub[:, k, :], in0=xn[:, k, :], scalar=sub_g[:, :],
                                                 in1=sub_rstd[j][:, (k % 2) * T:(k % 2 + 1) * T], op0=ALU.mult,
                                                 op1=ALU.mult).then_inc(cs_t, 1)

                def lows(ks):
                    for k in ks:
                        dve.wait_ge(cs_hi_ready, 8 + k + 1)
                        low(cs_lo[:, k, :], ub[:, k, :], cs_hi[:, k, :]).then_inc(cs_ready, 1)

                dve.wait_ge(ev("bias_in"), 32)
                pair(0, False)
                with dve.Fori(1, 4) as i:
                    pair(i, True)
                scored(3, 0)
                sub_norm(0)
                weights(3, 0)
                scored(3, 1)
                sub_norm(1)
                weights(3, 1)
                sub_norm(2)
                lows(range(6))
                sub_norm(3)
                lows(range(6, 8))
                split(c + 16)
                split(c + 17)
                projected(n, c + 12)

            def gating(n):
                c = BASE[n]
                dve.wait_ge(ev("sgu_in"), 64)
                dve.tensor_tensor(w_mix, w_mix, causal.unsqueeze(1).to_broadcast([P, KT, P]), ALU.mult)\
                    .then_inc(ev("w_mix"), 1)
                for j in range(5):
                    split(c + 2 + j)
                dve.wait_ge(ev("v_gelu"), 4)
                link(dve.tensor_reduce(v_sum, v_g, AX_X, ALU.add))
                link(dve.tensor_scalar(v_mean, v_sum, 1.0 / D, None, ALU.mult))
                for t in range(2):
                    dve.tensor_scalar(v_g[:, t, :], v_g[:, t, :], v_mean[:, t:t + 1], None, ALU.subtract)\
                        .then_inc(ev("v_centred"), 1)
                split(c + 7)
                dve.wait_ge(ev("v_rt"), 1)
                link(dve.reciprocal(v_rstd, v_rt))
                for t in range(2):
                    dve.scalar_tensor_tensor(out=v_g[:, t, :], in0=v_g[:, t, :], scalar=v_rstd[:, t:t + 1],
                                             in1=ln_rows[:, 0, :], op0=ALU.mult, op1=ALU.mult).then_inc(ev("v_scaled"), 1)
                for t in range(2):
                    dve.wait_ge(ev("v_scaled"), t + 1)
                    dve.tensor_tensor(v_g[:, t, :], v_g[:, t, :], ln_rows[:, 1, :], ALU.add).then_inc(ev("v_norm"), 1)
                split(c + 8)
                split(c + 9)
                split(c + 10)

                def lower(k):
                    dve.wait_ge(cs_hi_ready, 16 + k + 1)
                    low(cs_lo[:, k, :], xn[:, k, :], cs_hi[:, k, :]).then_inc(cs_ready, 1)

                for j in range(4):
                    dve.wait_ge(ev("mixed"), j + 1)
                    for k in (2 * j, 2 * j + 1):
                        dve.tensor_tensor(xn[:, k, :], bank[j][:, (k % 2) * T:(k % 2 + 1) * T], ub[:, k, :], ALU.mult)\
                            .then_inc(cs_t, 1)
                    for k in range(2 * j - 2, 2 * j) if j else ():
                        lower(k)
                lower(KT - 2)
                lower(KT - 1)
                split(c + 11)
                split(c + 12)
                split(c + 13)
                projected(n, c + 8)

            dve.wait_ge(memsets, 8)
            for n, (kind, _) in enumerate(STAGES):
                if n in (5, 9):
                    modulation(n // 9)
                if kind != "ple":
                    norm(n)
                {"ffn": ffn, "mix": mix, "ple": ple, "attn": attention, "sgu": gating, "renorm": lambda n: None}[kind](n)

        @block.tensor
        def _(pe):
            def mm3(out_, a_hi, a_lo, b_hi, b_lo, start, stop):
                pe.matmul(out_, a_hi, b_hi, start=start, stop=False, skip_group_check=True)
                pe.matmul(out_, a_hi, b_lo, start=False, stop=False, skip_group_check=True)
                return pe.matmul(out_, a_lo, b_hi, start=False, stop=stop, skip_group_check=True)

            def arrived(c, i=0):
                done, value = low_done(c)
                pe.wait_ge(done, value + 3 * i)

            def wide(s, b, hi, lo, each=None):
                wh, wl = lin(s, w_hi), lin(s, w_lo)
                order = [(k, nb) for nb in range(2) for k in range(KT)] if each is None else \
                    [(k, nb) for k in range(KT) for nb in range(2)]
                for k, nb in order:
                    if each is not None and nb == 0:
                        pe.wait_ge(each[0], each[1] + k + 1)
                    ins = mm3(bank[b][:, nb * T:(nb + 1) * T], wh[:, k, nb * P:(nb + 1) * P],
                              wl[:, k, nb * P:(nb + 1) * P], hi[:, k, :], lo[:, k, :],
                              k == 0 and nb == 0, k == KT - 1)
                ins.then_inc(chunks_done, 1)

            def token_major(s, b, each=None):
                wh, wl = lin(s, w_hi), lin(s, w_lo)
                for k in range(KT):
                    if each is not None:
                        pe.wait_ge(each[0], each[1] + k + 1)
                    for t in range(2):
                        ins = mm3(bank[b][:, t * NC:(t + 1) * NC], xs_hi[:, k, t * P:(t + 1) * P],
                                  xs_lo[:, k, t * P:(t + 1) * P], wh[:, k, :], wl[:, k, :],
                                  k == 0 and t == 0, k == KT - 1)
                ins.then_inc(chunks_done, 1)

            def over_two(s, hi, lo, first, last, f=None, between=None):
                wh, wl = tail(s, w_hi), tail(s, w_lo)
                for nb in range(KT):
                    o = bank[nb // 2][:, (nb % 2) * T:(nb % 2 + 1) * T]
                    for j in range(2):
                        ins = mm3(o, wh[:, j, nb * P:(nb + 1) * P], wl[:, j, nb * P:(nb + 1) * P],
                                  hi(j), lo(j), first and j == 0 and nb % 2 == 0, last and j == 1)
                    if last and f is not None and nb % 2 and nb < KT - 1:
                        ins.then_inc(bank_done, 1)
                    if nb == 1 and between is not None:
                        between()
                ins.then_inc(chunks_done, 1)

            def norm(n, after=False):
                if n and not after:
                    pe.wait_ge(consts_in, 16)
                for k in [0, 2, 4, 6, 7] if PAIRED[n] else range(KT):
                    if PAIRED[n] and k < 6:
                        pe.wait_ge(sq_added, 3 * PAIRED_NO[n] + k // 2 + 1)
                    else:
                        pe.wait_ge(sq_ready, 8 * n + k + 1)
                    ins = pe.matmul(bank[STAT][:, 0:T], ones_d[:, :], xn[:, k, :], start=(k == 0), stop=(k == KT - 1),
                                    skip_group_check=True)
                ins.then_inc(ss_ready, 1)
                if n and not after:
                    for _ in range(FILL):
                        pe.matmul(bank[MISC][:, :], ones_d[:, :], consts[:, 0:4, :], start=True, stop=True,
                                  skip_group_check=True)

            def ffn(n):
                f, c0 = FFN_NO[n], BASE[n]
                s0 = STEPS * f
                xw = (xs_ready, 8 * SPLIT_NO[n])
                g_half = (lambda j: gu_hi[:, j * T:(j + 1) * T]), (lambda j: gu_lo[:, j * T:(j + 1) * T])

                arrived(c0)
                wide(c0 % SLOTS, GATE, xs_hi, xs_lo, xw)
                if n == 0:
                    pe.wait_ge(ev("lam_prod"), 1)
                    pe.matmul(bank[MISC][:, SKEW:SKEW + 2], ones_1[0:64, :], lam_in[:, 4:6], start=True, stop=True,
                              skip_group_check=True).then_inc(ev("lam_sum"), 1)
                    pe.wait_ge(ev("table_in"), 32)
                    pe.matmul(bank[MISC][0:HA, 0:SKEW], table, one_hot, start=False, stop=True, skip_group_check=True)\
                        .then_inc(ev("rows_mm"), 1)
                arrived(c0 + 1)
                wide((c0 + 1) % SLOTS, UP, xs_hi, xs_lo)
                arrived(c0 + 2)
                pe.wait_ge(silu_done, s0 + 1)
                wide((c0 + 2) % SLOTS, GATE, xs_hi, xs_lo)
                arrived(c0 + 3)
                pe.wait_ge(gu_ready, s0 + 1)
                wide((c0 + 3) % SLOTS, UP, xs_hi, xs_lo)
                arrived(c0 + 4)
                pe.wait_ge(gulo_ready, s0 + 1)
                over_two((c0 + 4) % SLOTS, *g_half, True, False)
                cl = c0 + 5
                with pe.Fori(0, LOOPED) as i:
                    arrived(cl, i)
                    pe.wait_ge(silu_done, s0 + 2 + i)
                    wide(cl % SLOTS, GATE, xs_hi, xs_lo)
                    arrived(cl + 1, i)
                    pe.wait_ge(gu_ready, s0 + 2 + i)
                    wide((cl + 1) % SLOTS, UP, xs_hi, xs_lo)
                    arrived(cl + 2, i)
                    pe.wait_ge(gulo_ready, s0 + 2 + i)

                    def ada_sum():
                        pe.wait_ge(ada_step, 8 * LOOPED * f + 8 + 8 * i)
                        for j in range(4):
                            ins = pe.matmul(bank[MISC][:, j:j + 1], ada_acc[:, j * P:(j + 1) * P], ones_1[:, 0:1],
                                            start=True, stop=True, skip_group_check=True)
                        ins.then_inc(ada_summed, 1)

                    over_two((cl + 2) % SLOTS, *g_half, False, False, between=ada_sum if f < 4 else None)
                arrived(c0 + 32)
                pe.wait_ge(gulo_ready, s0 + STEPS)
                over_two((c0 + 32) % SLOTS, lambda j: cs_hi[:, 6 + j, :], lambda j: cs_lo[:, 6 + j, :], False, True, f)

            def part_wide(s, b, ks, ready, first):
                wh, wl = lin(s, w_hi), lin(s, w_lo)
                for nb in range(2):
                    for k in ks:
                        if ready is not None and nb == 0:
                            pe.wait_ge(cs_ready, ready(k))
                        ins = mm3(bank[b][:, nb * T:(nb + 1) * T], wh[:, k, nb * P:(nb + 1) * P],
                                  wl[:, k, nb * P:(nb + 1) * P], cs_hi[:, k, :], cs_lo[:, k, :],
                                  first and nb == 0 and k == ks[0], not first and k == ks[-1])
                return ins

            def outputs_in_parts(c, parts, early, late, ready, between):
                for j in range(parts):
                    arrived(c + j)
                    part_wide((c + j) % SLOTS, j, early, ready if j == 0 else None, True)
                    if j == 0 and between is not None:
                        between()
                for j in range(parts):
                    part_wide((c + j) % SLOTS, j, late, ready if j == 0 else None, False).then_inc(chunks_done, 1)
                for j in range(parts, 4):
                    arrived(c + j)
                    wide((c + j) % SLOTS, j, cs_hi, cs_lo)

            def outputs(c, cs, read=None):
                for j in range(4):
                    arrived(c + j)
                    if read is not None:
                        pe.wait_ge(read[0], read[1] + 2 * j + 2)
                    wide((c + j) % SLOTS, j, cs_hi, cs_lo, (cs_ready, cs) if j == 0 else None)

            def mix(n):
                c = BASE[n]
                pe.wait_ge(consts_in, 16)
                for j in range(10):
                    arrived(c + j)
                    if j in (6, 7):
                        pe.wait_ge(ev("glu_done"), 1)
                        token_major((c + j) % SLOTS, j - 6)
                    else:
                        if j in (8, 9):
                            pe.wait_ge(ev("glu_done"), 2)
                        wide((c + j) % SLOTS, (1, 0, 3, 2, 4, 5, None, None, 2, 3)[j], xs_hi, xs_lo,
                             (xs_ready, 8 * SPLIT_NO[n]) if j == 0 else None)
                    if j == 5:
                        pe.wait_ge(ev("gate_w_in"), 48)
                        for k in range(KT):
                            ins = pe.matmul(bank[MISC][0:16, 0:T], w_glr[:, k, :], xn[:, k, :], start=(k == 0),
                                            stop=(k == KT - 1), skip_group_check=True)
                        ins.then_inc(ev("glr_done"), 1)
                    if j == 6:
                        pe.wait_ge(ev("glr_copied"), 1)
                        for t in range(2):
                            ins = pe.matmul(bank[STAT][:, t * T:(t + 1) * T], glr[0:17, t * P:(t + 1) * P], wup[0:17, :],
                                            start=(t == 0), stop=True, skip_group_check=True)
                        ins.then_inc(ev("z_done"), 1)
                    if j == 7:
                        pe.wait_ge(ev("log_a"), 1)
                        for h in range(2):
                            for t in range(2):
                                ins = pe.matmul(bank[MISC][:, h * T + t * P:h * T + (t + 1) * P],
                                                log_a[:, t * T + h * P:t * T + (h + 1) * P], tri,
                                                start=(h == 0 and t == 0), stop=True, skip_group_check=True)
                        ins.then_inc(ev("cum_done"), 1)
                pe.wait_ge(ev("k_end"), 1)
                pe.wait_ge(ev("log_a"), 1)
                for t in range(2):
                    for h in range(2):
                        ins = pe.matmul(bank[STAT][:, t * T + h * P:t * T + (h + 1) * P],
                                        k_end[:, h * T + t * P:h * T + (t + 1) * P], ident, is_transpose=True,
                                        start=(t == 0 and h == 0), stop=True, skip_group_check=True)
                ins.then_inc(ev("ke_turned"), 1)
                pe.wait_ge(ev("qk_scaled"), 4)
                pe.wait_ge(ev("silu_r"), 2)
                for par in range(2):
                    r = slice(64 * par, 64 * par + 64)
                    for b, k_, q_ in ((4 + par, k_neg, q_dec), (2 + par, k_pos, q_neg)):
                        for hh in range(2):
                            for t in range(2):
                                at = hh * T + t * P
                                ins = pe.matmul(bank[b][:, at:at + P], k_[r, at:at + P], q_[r, at:at + P],
                                                start=(hh == 0 and t == 0), stop=True, skip_group_check=True)
                    ins.then_inc(ev("scored"), 1)
                pe.wait_ge(ev("ke_copied"), 1)
                pe.wait_ge(ev("v_copied"), 2)
                for i in range(3):
                    r = slice(CHUNK * (i % 2), CHUNK * (i % 2) + CHUNK)
                    for h in range(HG):
                        o = bank[i % 2][64 * (h % 2):64 * (h % 2) + 64, (i // 2) * T + (h // 2) * P:(i // 2) * T + (h // 2 + 1) * P]
                        ins = pe.matmul(o, ke_t[r, i // 2, h * 64:(h + 1) * 64],
                                        v_tok[r, h // 2, i // 2, (h % 2) * P:(h % 2 + 1) * P],
                                        start=(i < 2 and h < 2), stop=True, skip_group_check=True)
                ins.then_inc(ev("kv_done"), 1)
                for par in range(2):
                    r = slice(64 * par, 64 * par + 64)
                    pe.wait_ge(ev("score_sel"), 2 * par + 2)
                    for hh in range(2):
                        for t in range(2):
                            pe.matmul(bank[6 + par][:, hh * T + t * P:hh * T + (t + 1) * P],
                                      v_tok[:, hh, t, par * P:(par + 1) * P], score[par][:, 2 * hh + t, :],
                                      start=(hh == 0 and t == 0), stop=False, skip_group_check=True)
                    pe.wait_ge(ev("state"), 5)
                    for hh in range(2):
                        for i in range(1, 4):
                            at = hh * T + i * CHUNK
                            ins = pe.matmul(bank[6 + par][:, at:at + CHUNK], state[r, i - 1, hh, :],
                                            q_dec[r, at:at + CHUNK], start=False, stop=True, skip_group_check=True)
                    ins.then_inc(ev("o_done"), 1)
                for par in range(2):
                    pe.wait_ge(ev("o_sq"), par + 1)
                    pe.matmul(bank[4 + par][:, :], ones_v[:, :], ub[:, 4 + 2 * par:6 + 2 * par, :], start=True, stop=True,
                              skip_group_check=True).then_inc(ev("o_ms"), 1)
                pe.wait_ge(ev("conv_step"), CT * CONV)
                for k in range(CT):
                    ins = pe.matmul(bank[3][:, 0:T], ones_c[:, :], conv_y[:, k, :], start=(k == 0), stop=(k == CT - 1),
                                    skip_group_check=True)
                ins.then_inc(ev("ln_mean"), 1)

                def variance():
                    pe.wait_ge(ev("ln_sq"), 1)
                    for k in range(CT):
                        ins = pe.matmul(bank[3][:, T:2 * T], ones_c[:, :], conv_y[:, k, :], start=(k == 0),
                                        stop=(k == CT - 1), skip_group_check=True)
                    ins.then_inc(ev("ln_var"), 1)

                outputs_in_parts(c + 10, 3, range(4, KT), range(4), lambda k: k - 3 if k >= 4 else k + 5, variance)

            def ple(n):
                c = BASE[n]
                norm(n, True)
                pe.wait_ge(ev("p_lo"), 1)
                arrived(c)
                over_two(c % SLOTS, lambda j: cs_hi[:, j, :], lambda j: cs_lo[:, j, :], True, True)
                for j in range(4):
                    arrived(c + 1 + j)
                    if j >= 2:
                        pe.wait_ge(ev("ple_sig"), j - 1)
                    wide((c + 1 + j) % SLOTS, 4 + j % 2, xs_hi, xs_lo, (xs_ready, 8 * SPLIT_NO[n]) if j == 0 else None)

            def attention(n):
                c = BASE[n]

                def logits(i, j):
                    e = 2 * i + j
                    pe.wait_ge(ev("qk_n"), 2 * i + 2)
                    if not (isinstance(i, int) and i == 0 and j == 0):
                        pe.wait_ge(ev("logit"), 2 * e)
                    for comp in range(2):
                        r = slice(64 * comp, 64 * comp + 64)
                        pe.matmul(bank[4 + comp][:, 0:P], q_n[r, j * T:j * T + P], k_n[r, j * T:j * T + P],
                                  start=True, stop=True, skip_group_check=True)
                        ins = pe.matmul(bank[4 + comp][:, P:SKEW], q_n[r, j * T + P:(j + 1) * T], k_n[r, j * T:(j + 1) * T],
                                        start=False, stop=True, skip_group_check=True)
                    ins.then_inc(ev("logits"), 1)

                def turn(i, j):
                    e = 2 * i + j
                    pe.wait_ge(ev("attn"), 2 * e + 2)
                    for m in range(3):
                        ins = pe.matmul(bank[MISC][:, m * P:(m + 1) * P], attn[:, m * P:(m + 1) * P], ident,
                                        is_transpose=True, start=(m == 0), stop=True, skip_group_check=True)
                    ins.then_inc(ev("turned"), 1)

                def out(i, j):
                    e = 2 * i + j
                    pe.wait_ge(ev("turned_copied"), e + 1)
                    pe.wait_ge(ev("va"), i + 1)
                    if j == 0 and not (isinstance(i, int) and i == 0):
                        pe.wait_ge(ev("o_copied"), i)
                    v = lambda t: va[:, t, j * P:(j + 1) * P]
                    o = bank[7]
                    pe.matmul(o[:, j * T:j * T + P], v(0), attn_t[:, 0:P], start=(j == 0), stop=True, skip_group_check=True)
                    pe.matmul(o[:, j * T + P:(j + 1) * T], v(0), attn_t[:, P:2 * P], start=False, stop=False,
                              skip_group_check=True)
                    ins = pe.matmul(o[:, j * T + P:(j + 1) * T], v(1), attn_t[:, 2 * P:3 * P], start=False, stop=True,
                                    skip_group_check=True)
                    if j == 1:
                        ins.then_inc(ev("pair_done"), 1)

                def square_sums(i, which):
                    pe.wait_ge(ev("qk_sq"), 2 * i + which + 1)
                    if which:
                        pe.wait_ge(ev("qk_log"), 2 * i + 1)
                    pe.matmul(bank[3][:, :], pair_ones, qk_sq, start=True, stop=True, skip_group_check=True)\
                        .then_inc(ev("qk_norm_ms"), 1)

                def chunk(i, part, first=False):
                    arrived(c + part, i)
                    s = (c + part) % SLOTS
                    if part < 2:
                        if not first:
                            pe.wait_ge(ev("qk_raw"), 2 * i + part - 1)
                            pe.wait_ge(ev("qk_sq"), 2 * i + part - 1)
                        wide(s, part, xs_hi, xs_lo, (xs_ready, 8 * SPLIT_NO[n]) if first and part == 0 else None)
                    else:
                        if not first:
                            pe.wait_ge(ev("va"), i)
                        token_major(s, 2)

                def pair(i, before):
                    chunk(i, 0, not before)
                    if before:
                        logits(i - 1, 0)
                    chunk(i, 1, not before)
                    square_sums(i, 0)
                    if before:
                        logits(i - 1, 1)
                        turn(i - 1, 0)
                    chunk(i, 2, not before)
                    if before:
                        out(i - 1, 0)
                        turn(i - 1, 1)
                        out(i - 1, 1)
                    square_sums(i, 1)

                def sub_sums(j):
                    pe.wait_ge(ev("sub_sq"), j + 1)
                    if j >= 2:
                        pe.wait_ge(ev("sub_kept"), 2 * j - 3)
                    pe.matmul(bank[SUB_BANK[j]][:, :], ones_v[:, :], ub[:, 2 * j:2 * j + 2, :], start=True, stop=True,
                              skip_group_check=True).then_inc(ev("sub_ms"), 1)

                pair(0, False)
                with pe.Fori(1, 4) as i:
                    pair(i, True)
                logits(3, 0)
                pe.wait_ge(ev("qk_log"), 8)
                sub_sums(0)
                pe.wait_ge(ev("va"), 4)
                sub_sums(1)
                logits(3, 1)
                sub_sums(2)
                turn(3, 0)
                out(3, 0)
                turn(3, 1)
                out(3, 1)
                outputs_in_parts(c + 12, 2, range(6), range(6, KT), lambda k: 8 + k + 1, lambda: sub_sums(3))

            def gating(n):
                c = BASE[n]
                for j in range(4):
                    arrived(c + j)
                    token_major((c + j) % SLOTS, j, (xs_ready, 8 * SPLIT_NO[n]) if j == 0 else None)
                for j in range(4):
                    arrived(c + 4 + j)
                    if j >= 2:
                        pe.wait_ge(ev("u_gelu"), j - 1)
                    wide((c + 4 + j) % SLOTS, 4 + j % 2, xs_hi, xs_lo)
                pe.wait_ge(ev("w_mix"), 1)
                pe.wait_ge(ev("v_norm"), 2)
                for g in range(KT):
                    for t in range(2):
                        o = bank[g // 2][:, (g % 2) * T + t * P:(g % 2) * T + (t + 1) * P]
                        pe.matmul(o, v_g[:, t, g * P:(g + 1) * P], w_mix[:, g, :], start=(g % 2 == 0 and t == 0), stop=False,
                                  skip_group_check=True)
                        ins = pe.matmul(o, ones_1[0:1, :], b_mix[:, g, :], start=False, stop=True, skip_group_check=True)
                    if g % 2:
                        ins.then_inc(ev("mixed"), 1)
                outputs(c + 8, 16, (cs_t, 12))

            pe.wait_ge(memsets, 8)
            for n, (kind, _) in enumerate(STAGES):
                if kind != "ple":
                    norm(n)
                {"ffn": ffn, "mix": mix, "ple": ple, "attn": attention, "sgu": gating, "renorm": lambda n: None}[kind](n)


def shape_constants():
    s, t = np.arange(P)[:, None], np.arange(P)[None, :]
    same = s // CHUNK == t // CHUNK
    consts = np.stack([
        np.where(same & (s <= t), 1 / 16, 0), same & (s <= t), same & (s > t), s == t, s <= t,
        np.where(s // 64 == t // 64, 1 / 64, 0),
    ], 1).astype(np.float32)
    one_hot = np.zeros((NB + 1, SKEW), np.float32)
    for m in range(SKEW):
        rel = T - 1 - m
        if rel < 0:
            b = NB
        elif rel < 16:
            b = rel
        else:
            b = min(NB - 1, 16 + int(np.floor(np.log2(rel / 16) / 3 * 16 + 1e-9)))
        one_hot[b, m] = 1
    return consts, one_hot


def kernel(**inputs):
    import concourse.bacc as bacc
    from concourse.bass_utils import run_bass_kernel_spmd

    a = {k: np.asarray(v) for k, v in inputs.items()}

    def tiles(v):
        v = v.reshape(-1, P)
        return v.T

    parts = {k: a[k] for k in COLS}
    parts["conv_w"] = a["conv_w"][0].T.reshape(CT, P, CONV).transpose(0, 2, 1)
    for k in ("attn_q_norm_2", "attn_k_norm_2"):
        parts[k] = np.concatenate([a[k][0], a[k][0]])
    consts, one_hot = shape_constants()
    arrays = {
        "x": a["x"][0].reshape(T, KT, P).transpose(2, 1, 0),
        "p": a["p"][0, 0].reshape(T, 2, P).transpose(2, 1, 0),
        "cols": np.concatenate([tiles(parts[k]) for k in COLS], 1),
        "lam": np.stack([a[k][0] for k in ("attn_lq1_2", "attn_lk1_2", "attn_lq2_2", "attn_lk2_2")], 1),
        "w_mix": a["sgu_w_s_2"][0].transpose(2, 0, 1),
        "consts": consts,
        "one_hot": one_hot,
    }
    for k in ("ffn1_w_in", "ffn1_w_out", "ffn2_w_in", "ffn2_w_out", "w_in", "w_out", "gate_w_up", "gate_b",
              "ple_w_gate", "ple_w_proj", "rel_bias_2", "ada_w_2", "ffn1_wg_2", "ffn1_wu_2", "ffn1_wd_2",
              "ffn2_wg_2", "ffn2_wu_2", "ffn2_wd_2", "attn_w_qkv_2", "attn_w_o_2", "sgu_w_in_2", "sgu_w_out_2",
              "sgu_ln_g_2", "sgu_ln_b_2", "sgu_b_s_2"):
        arrays[k] = a[k]
    arrays = {f"in_{k}": np.ascontiguousarray(v) for k, v in arrays.items()}
    nc = bacc.Bacc("TRN2", target_bir_lowering=False, num_devices=1)
    dram = {k[3:]: nc.dram_tensor(k, v.shape, mybir.dt.from_np(v.dtype), kind="ExternalInput").ap()
            for k, v in arrays.items()}
    out = nc.dram_tensor("out", (P, KT, T), F32, kind="ExternalOutput").ap()
    two_blocks(nc, dram, out)
    got = run_bass_kernel_spmd(nc, [arrays], core_ids=[0]).results[0]["out"]
    return got.reshape(P, KT, T).transpose(2, 1, 0).reshape(1, T, D)
```
